# Optimizing a Trainium2 kernel written in Bass

```python
import math
import jax, jax.numpy as jnp
from jax import lax
import numpy as np

D_MODEL = 1024
BATCH = 1
SEQ = 1024
DEPTH = 1
DEC_BATCH = 1
DEC_SEQ = 64
PAST_LEN = 128

CHUNK = 64
D_CONV = D_MODEL
CONV_W = 31
D_GMLP = D_MODEL
GMLP_CHUNK = 128
GMLP_GROUPS = 8
GMLP_GW = D_GMLP // GMLP_GROUPS
N_HEADS = 8
HEAD_DIM = 128
N_KV = 2
GQA_G = N_HEADS // N_KV
IDX_HEADS = 8
IDX_DIM = 64
TOPK_MAX = 256
Q_BLOCK = 128
D_FF = 4 * D_MODEL
N_BRANCH = 3
EPS = 1e-6
IN_SPLIT = (2 * D_CONV, 2 * D_GMLP, N_HEADS * HEAD_DIM, N_KV * HEAD_DIM, N_KV * HEAD_DIM,
            IDX_HEADS * IDX_DIM, IDX_DIM, IDX_HEADS, N_BRANCH * D_MODEL)
IN_COLS = 2 * D_CONV + 2 * D_GMLP + N_HEADS * HEAD_DIM + 2 * N_KV * HEAD_DIM + IDX_HEADS * IDX_DIM + IDX_DIM + IDX_HEADS + N_BRANCH * D_MODEL

kernel_name = 'hybrid_stream_conv_gmlp_dsa_step'

def rms_norm(x, g):
    xf = x.astype(jnp.float32)
    y = xf * lax.rsqrt(jnp.mean(xf * xf, axis=-1, keepdims=True) + EPS)
    return (y * g).astype(x.dtype)

def layer_norm(x, g, b):
    xf = x.astype(jnp.float32)
    mu = jnp.mean(xf, axis=-1, keepdims=True)
    var = jnp.mean(jnp.square(xf - mu), axis=-1, keepdims=True)
    return ((xf - mu) * lax.rsqrt(var + EPS) * g + b).astype(x.dtype)

def split_cols(p):
    out, start = [], 0
    for n in IN_SPLIT:
        out.append(p[..., start:start + n])
        start += n
    return out

def causal_dwconv(xpad, w, b):
    y = lax.conv_general_dilated(xpad, w[:, None, :], window_strides=(1,), padding='VALID',
                                 dimension_numbers=('NWC', 'WIO', 'NWC'),
                                 feature_group_count=xpad.shape[-1])
    return y + b

def spatial_gate(v, w_s, b_s, L):
    B, T, _ = v.shape
    vb = v.reshape(B, T // L, L, GMLP_GROUPS, GMLP_GW)
    mask = jnp.tril(jnp.ones((L, L), dtype=bool))
    wm = jnp.where(mask[None], w_s[:, :L, :L], 0)
    s = jnp.einsum('gij,bcjge->bcige', wm, vb)
    s = s + jnp.swapaxes(b_s[:, :L], 0, 1)[None, None, :, :, None]
    return s.reshape(B, T, D_GMLP)

def sparse_attention(q, k, v, qi, ki, wi, q_pos, topk, block):
    B, T = q.shape[0], q.shape[1]
    S = k.shape[1]
    nb = T // block
    k_chunk = jnp.arange(S, dtype=jnp.int32) // CHUNK
    slopes = jnp.exp2(-8.0 * jnp.arange(1, N_HEADS + 1, dtype=jnp.float32) / N_HEADS).reshape(N_KV, GQA_G)
    gather = jax.vmap(lambda a, i: a[i])

    def to_blocks(a):
        return jnp.swapaxes(a.reshape((B, nb, block) + a.shape[2:]), 0, 1)

    def one_block(args):
        qb, qib, wib, pb = args
        dots = jnp.einsum('bqhd,bsd->bqhs', qib, ki, preferred_element_type=jnp.float32) * IDX_DIM ** -0.5
        score = jnp.einsum('bqh,bqhs->bqs', wib.astype(jnp.float32), jax.nn.relu(dots))
        vis = k_chunk[None, :] <= (pb // CHUNK)[:, None]
        score = jnp.where(vis[None], score, -jnp.inf)
        top_val, top_idx = lax.top_k(score, topk)
        valid = jnp.isfinite(top_val)
        ks = gather(k, top_idx)
        vs = gather(v, top_idx)
        qg = qb.reshape(B, block, N_KV, GQA_G, HEAD_DIM)
        logits = jnp.einsum('bqngd,bqknd->bqngk', qg, ks, preferred_element_type=jnp.float32) * HEAD_DIM ** -0.5
        dist = jnp.abs(pb[None, :, None] - top_idx).astype(jnp.float32)
        logits = logits - slopes[None, None, :, :, None] * dist[:, :, None, None, :]
        logits = jnp.where(valid[:, :, None, None, :], logits, -jnp.inf)
        p = jax.nn.softmax(logits, axis=-1).astype(v.dtype)
        o = jnp.einsum('bqngk,bqknd->bqngd', p, vs)
        return o.reshape(B, block, N_HEADS * HEAD_DIM)

    out = lax.map(one_block, (to_blocks(q), to_blocks(qi), to_blocks(wi), q_pos.reshape(nb, block)))
    return jnp.swapaxes(out, 0, 1).reshape(B, T, N_HEADS * HEAD_DIM)

def trunk_layer(x, c, q_pos, cache, W):
    B, T, D = x.shape
    mod = jax.nn.silu(c) @ W['w_ada'] + W['b_ada']
    sh1, sc1, g1, sh2, sc2, g2 = jnp.split(mod[:, None, :], 6, axis=-1)
    h = rms_norm(x, W['g_norm1']) * (1 + sc1) + sh1
    a_in, b_in, q, k, v, qi, ki, wi, gl = split_cols(h @ W['w_in'])

    a = a_in[..., :D_CONV] * jax.nn.sigmoid(a_in[..., D_CONV:])
    hist = jnp.zeros((B, CONV_W - 1, D_CONV), a.dtype) if cache is None else cache[3]
    apad = jnp.concatenate([hist, a], axis=1)
    new_conv = apad[:, -(CONV_W - 1):]
    a = causal_dwconv(apad, W['w_dw'], W['b_dw'])
    y_a = jax.nn.silu(layer_norm(a, W['ln_c_g'], W['ln_c_b'])) @ W['w_pa']

    z = jax.nn.gelu(b_in)
    u = z[..., :D_GMLP]
    vg = layer_norm(z[..., D_GMLP:], W['ln_v_g'], W['ln_v_b'])
    L = GMLP_CHUNK if cache is None else T
    y_b = (u * spatial_gate(vg, W['w_s'], W['b_s'], L)) @ W['w_pb']

    q = rms_norm(q.reshape(B, T, N_HEADS, HEAD_DIM), W['g_q'])
    k = rms_norm(k.reshape(B, T, N_KV, HEAD_DIM), W['g_k'])
    v = v.reshape(B, T, N_KV, HEAD_DIM)
    qi = qi.reshape(B, T, IDX_HEADS, IDX_DIM)
    wi = wi * IDX_HEADS ** -0.5
    if cache is None:
        k_all, v_all, ki_all = k, v, ki
    else:
        k_all = jnp.concatenate([cache[0], k], axis=1)
        v_all = jnp.concatenate([cache[1], v], axis=1)
        ki_all = jnp.concatenate([cache[2], ki], axis=1)
    S = k_all.shape[1]
    topk = min(TOPK_MAX, S // 4)
    o = sparse_attention(q, k_all, v_all, qi, ki_all, wi, q_pos, topk, min(Q_BLOCK, T))
    y_c = o @ W['w_pc']

    gates = jax.nn.sigmoid(gl).reshape(B, T, N_BRANCH, D)
    m = gates[:, :, 0] * y_a + gates[:, :, 1] * y_b + gates[:, :, 2] * y_c
    x = x + g1 * (m @ W['w_o'])

    h2 = rms_norm(x, W['g_norm2']) * (1 + sc2) + sh2
    f = jnp.square(jax.nn.relu(h2 @ W['w_1'] + W['b_1'])) @ W['w_2'] + W['b_2']
    x = x + g2 * f
    return x, (k, v, ki, new_conv, vg)

def setup_inputs(seed: int = 0) -> dict:
    key = jax.random.key(seed)
    ks = iter(jax.random.split(key, 40))
    nrm = lambda shape, scale: scale * jax.random.normal(next(ks), shape, jnp.float32)
    D = D_MODEL
    return {
        'x_prompt': nrm((BATCH, SEQ, D), 1.0),
        'x_sample': nrm((DEC_BATCH, DEC_SEQ, D), 1.0),
        'c_prompt': nrm((BATCH, D), 1.0),
        'c_sample': nrm((DEC_BATCH, D), 1.0),
        'cache_k': nrm((DEPTH, DEC_BATCH, PAST_LEN, N_KV, HEAD_DIM), 1.0),
        'cache_v': nrm((DEPTH, DEC_BATCH, PAST_LEN, N_KV, HEAD_DIM), 1.0),
        'cache_kidx': nrm((DEPTH, DEC_BATCH, PAST_LEN, IDX_DIM), 1.0),
        'cache_conv': nrm((DEPTH, DEC_BATCH, CONV_W - 1, D_CONV), 0.5),
        'w_ada': nrm((DEPTH, D, 6 * D), 0.5 * D ** -0.5),
        'b_ada': nrm((DEPTH, 6 * D), 0.1),
        'g_norm1': 1.0 + nrm((DEPTH, D), 0.05),
        'w_in': nrm((DEPTH, D, IN_COLS), D ** -0.5),
        'w_dw': nrm((DEPTH, CONV_W, D_CONV), CONV_W ** -0.5),
        'b_dw': nrm((DEPTH, D_CONV), 0.02),
        'ln_c_g': 1.0 + nrm((DEPTH, D_CONV), 0.05),
        'ln_c_b': nrm((DEPTH, D_CONV), 0.02),
        'w_pa': nrm((DEPTH, D_CONV, D), D_CONV ** -0.5),
        'ln_v_g': 1.0 + nrm((DEPTH, D_GMLP), 0.05),
        'ln_v_b': nrm((DEPTH, D_GMLP), 0.02),
        'w_s': nrm((DEPTH, GMLP_GROUPS, GMLP_CHUNK, GMLP_CHUNK), GMLP_CHUNK ** -0.5),
        'b_s': 1.0 + nrm((DEPTH, GMLP_GROUPS, GMLP_CHUNK), 0.1),
        'w_pb': nrm((DEPTH, D_GMLP, D), D_GMLP ** -0.5),
        'g_q': 1.0 + nrm((DEPTH, HEAD_DIM), 0.05),
        'g_k': 1.0 + nrm((DEPTH, HEAD_DIM), 0.05),
        'w_pc': nrm((DEPTH, N_HEADS * HEAD_DIM, D), (N_HEADS * HEAD_DIM) ** -0.5),
        'w_o': nrm((DEPTH, D, D), D ** -0.5),
        'g_norm2': 1.0 + nrm((DEPTH, D), 0.05),
        'w_1': nrm((DEPTH, D, D_FF), D ** -0.5),
        'b_1': nrm((DEPTH, D_FF), 0.02),
        'w_2': nrm((DEPTH, D_FF, D), D_FF ** -0.5),
        'b_2': nrm((DEPTH, D), 0.02),
    }

def reference(x_prompt, x_sample, c_prompt, c_sample, cache_k, cache_v, cache_kidx, cache_conv,
              w_ada, b_ada, g_norm1, w_in, w_dw, b_dw, ln_c_g, ln_c_b, w_pa, ln_v_g, ln_v_b,
              w_s, b_s, w_pb, g_q, g_k, w_pc, w_o, g_norm2, w_1, b_1, w_2, b_2):
    pos_p = jnp.arange(x_prompt.shape[1], dtype=jnp.int32)
    pos_s = PAST_LEN + jnp.arange(x_sample.shape[1], dtype=jnp.int32)
    hp, hs = x_prompt, x_sample
    kp_l, vp_l, kip_l, cp_l = [], [], [], []
    ks_l, vs_l, kis_l, cs_l, gv_l = [], [], [], [], []
    for l in range(DEPTH):
        W = dict(w_ada=w_ada[l], b_ada=b_ada[l], g_norm1=g_norm1[l], w_in=w_in[l], w_dw=w_dw[l],
                 b_dw=b_dw[l], ln_c_g=ln_c_g[l], ln_c_b=ln_c_b[l], w_pa=w_pa[l], ln_v_g=ln_v_g[l],
                 ln_v_b=ln_v_b[l], w_s=w_s[l], b_s=b_s[l], w_pb=w_pb[l], g_q=g_q[l], g_k=g_k[l],
                 w_pc=w_pc[l], w_o=w_o[l], g_norm2=g_norm2[l], w_1=w_1[l], b_1=b_1[l], w_2=w_2[l],
                 b_2=b_2[l])
        hp, (kp, vp, kip, cp, _) = trunk_layer(hp, c_prompt, pos_p, None, W)
        hs, (ksn, vsn, kisn, csn, gvn) = trunk_layer(
            hs, c_sample, pos_s, (cache_k[l], cache_v[l], cache_kidx[l], cache_conv[l]), W)
        kp_l.append(kp); vp_l.append(vp); kip_l.append(kip); cp_l.append(cp)
        ks_l.append(ksn); vs_l.append(vsn); kis_l.append(kisn); cs_l.append(csn); gv_l.append(gvn)
    return (hp, hs,
            jnp.stack(kp_l), jnp.stack(vp_l), jnp.stack(kip_l), jnp.stack(cp_l),
            jnp.stack(ks_l), jnp.stack(vs_l), jnp.stack(kis_l), jnp.stack(cs_l), jnp.stack(gv_l))


_drawn_inputs = setup_inputs


def setup_inputs(seed=0):
    import zlib

    import numpy as np

    out = dict(_drawn_inputs(seed))
    spreads = {}
    factors = {'cache_k': 3.787,
     'cache_v': 2.789,
     'b_dw': 8.0,
     'ln_c_g': 8.0,
     'ln_c_b': 32.914,
     'ln_v_b': 2.909,
     'b_s': 4.396,
     'g_q': 8.0,
     'b_1': 6.128,
     'b_2': 47.329,
     'g_norm2': 3.456}
    for name, (base, spread) in spreads.items():
        noise = np.random.default_rng([zlib.crc32(name.encode()), seed]).standard_normal(out[name].shape)
        drawn = base * np.exp(spread * noise) if base else spread * noise
        out[name] = __import__('jax').numpy.asarray(drawn.astype(out[name].dtype))
    for name, factor in factors.items():
        out[name] = (out[name] * factor).astype(out[name].dtype)
    return out
```

```python
from contextlib import ExitStack

import concourse.bass as bass
from concourse import mybir

ALU = mybir.AluOpType
ACT = mybir.ActivationFunctionType
AX_X = mybir.AxisListType.X
F32 = mybir.dt.float32
F32R = mybir.dt.float32r
I32 = mybir.dt.int32

P = 128
D = 1024
KT = D // P
SEQ, DEC, PAST = 1024, 64, 128
TT = SEQ // P
CH = 3
CW = 364
NT = CH * CW
TOK = SEQ + DEC
CONV_W = 31
HIST = CONV_W - 1
APW = HIST + SEQ + HIST + DEC
CONV_N = APW - HIST
H, DH, NKV, G = 8, 128, 2, 4
IH, IDIM = 8, 64
CHUNK = 64
TOPK, TOPK_S = 256, 48
NKEY = SEQ + PAST + DEC
EPS = 1e-6
BIG = 1.0e30
LOW = -3.0e38
FF = 4 * D
FG = 4
NG = FF // P // FG

C_VAL, C_GATE, C_U, C_V = 0, D, 2 * D, 3 * D
C_Q = 4 * D
C_K = C_Q + H * DH
C_VV = C_K + NKV * DH
C_QI = C_VV + NKV * DH
C_KI = C_QI + IH * IDIM
KIW = IDIM + IH
C_GL = C_KI + KIW

N_KI = 0
N_QI = 1
N_GLU = N_QI + IH * IDIM // P
N_GATE = N_GLU + 2 * KT
N_KV = N_GATE + 3 * KT
N_Q = N_KV + 2 * NKV
N_VG = N_Q + H
N_U = N_VG + KT
N_PC = N_U + KT
N_PB = N_PC + KT
N_PA = N_PB + KT
N_WO = N_PA + KT
N_MLP = N_WO + KT
GT = FG + KT

R_GN1, R_BDW, R_LCG, R_LCB, R_LVG, R_LVB, R_GN2, R_B2 = (KT * i for i in range(8))
R_B1 = 8 * KT
R_GQ = R_B1 + FF // P
R_GK = R_GQ + 1
R_N = R_GK + 1
M_SH1, M_SC1, M_G1, M_SH2, M_SC2, M_G2 = (KT * i for i in range(6))
MODS = 6 * KT

STILES = list(range(2, TT)) + [TT]
WIDTH = [(t + 1) * P for t in range(TT)] + [PAST + DEC]
SOFF = {}
for _t in STILES:
    SOFF[_t] = sum(WIDTH[u] for u in STILES if u < _t)
SW = sum(WIDTH[t] for t in STILES)
NS = len(STILES)
BITS = 31


def kcol(t):
    return SEQ if t == TT else 0


def rows(t):
    return DEC if t == TT else P


def wait(eng, sem, value):
    if isinstance(value, int) and value <= 0:
        return
    eng.wait_ge(sem, value)


class Order:

    def __init__(self, eng, sem):
        self.eng, self.sem, self.n = eng, sem, 0

    def mark(self, ins):
        self.n += 1
        ins.then_inc(self.sem, 1)

    def settle(self):
        self.eng.wait_ge(self.sem, self.n)


def hybrid_stream_step(nc, x_prompt, x_sample, c_prompt, c_sample, cache_k, cache_v, cache_kidx, cache_conv,
                       w_ada, b_ada, g_norm1, w_in, w_dw, b_dw, ln_c_g, ln_c_b, w_pa, ln_v_g, ln_v_b,
                       w_s, b_s, w_pb, g_q, g_k, w_pc, w_o, g_norm2, w_1, b_1, w_2, b_2,
                       y_prompt, y_sample, new_k_p, new_v_p, new_ki_p, new_conv_p,
                       new_k_s, new_v_s, new_ki_s, new_conv_s, new_gv_s):
    with ExitStack() as ctx:
        def sem(name):
            return ctx.enter_context(nc.semaphore(name))

        base = 16640
        at = [base]

        def put(name, shape, dt=F32, offset=None):
            size = 4
            for s in shape[1:]:
                size *= s
            if offset is None:
                offset = at[0]
                at[0] += (size + 31) // 32 * 32
            return nc.alloc_sbuf_tensor_at(name, shape, dt, offset=offset)

        o_xa = at[0]
        xa = put("xa", [P, 2, KT, NT], F32R)
        x1T = put("x1T", [P, KT, NT], offset=o_xa)
        xf = put("xf", [P, 2, FG, NT], F32R, offset=o_xa + 4 * KT * NT)
        wada = put("wada", [P, 4, KT, 2 * P], offset=o_xa)
        o_b = at[0]
        xb = put("xb", [P, 2, KT, NT], F32R)
        at[0] = o_b
        score = put("score", [P, SW])
        o_ap = at[0]
        apad = put("apad", [P, KT, APW])
        xT = put("xT", [P, KT, NT], offset=o_ap)
        qiT = put("qiT", [P, IH * IDIM // P, NT], offset=o_ap)
        kiT = put("kiT", [P, NKEY], offset=o_ap + 4 * (IH * IDIM // P) * NT)
        zT = put("zT", [P, KT, NT], offset=o_ap)
        kT = put("kT", [P, NKV, NKEY])
        vtok = put("vtok", [P, TT + 2, NKV * DH])
        at[0] = max(at[0], o_b + 8 * KT * NT)
        raw = put("raw", [P, 2, KT, P])
        whi = put("whi", [P, 2, KT, P], F32R)
        wlo = put("wlo", [P, 2, KT, P], F32R)
        st = put("st", [P, 5, (TT + 1) * P])
        ident = put("ident", [P, P])
        mean_d = put("mean_d", [P, P])
        mean_h = put("mean_h", [P, P])
        dist = put("dist", [P, SEQ])
        dist01 = put("dist01", [P, 3 * P])
        wmT = put("wmT", [P, KT, P])
        o_q1 = at[0]
        qt = put("qt", [P, H, P])
        qt2 = put("qt2", [P, H, P], offset=o_q1 - 4 * KT * P)
        kiwi = put("kiwi", [P, TT + 1, KIW], offset=o_q1)
        par = put("par", [P, R_N])
        mod_b = put("mod_b", [P, MODS + 2 * KT])
        cT = put("cT", [P, 2, KT])
        mod = put("mod", [P, 2, MODS])
        gain1 = put("gain1", [P, 2, KT])
        gain2 = put("gain2", [P, 2, KT])
        b2g = put("b2g", [P, 2, KT])
        wdwT = put("wdwT", [P, KT, CONV_W])
        ctail = put("ctail", [P, KT, 2, HIST])
        wi = put("wi", [P, TT + 1, IH])
        eps = put("eps", [P, 1])
        gq = put("gq", [P, 1])
        one = put("one", [P, 1])
        ones_row = put("ones_row", [1, P])
        bs_row = put("bs_row", [1, KT, P], offset=o_q1)
        s_acc = put("s_acc", [P, NS], I32)
        s_flip = put("s_flip", [P, NS], I32)
        s_bit = put("s_bit", [P, 1], I32)
        s_take = put("s_take", [P, NS], I32)
        s_cand = put("s_cand", [P, NS], I32)
        s_cnt = put("s_cnt", [P, NS])
        mx = put("mx", [P, H])
        nmx = put("nmx", [P, H])
        rs = put("rs", [P, H])
        ri = put("ri", [P, H])
        assert at[0] <= nc.sbuf_usable_end, at[0]

        acc = ctx.enter_context(nc.psum_tensor("acc", [P, 2, CH, 512], F32))
        aux = ctx.enter_context(nc.psum_tensor("aux", [P, 2, 512], F32))

        xT_d = nc.dram_tensor("xT_d", [P, KT, NT], F32).ap()
        gate_d = nc.dram_tensor("gate_d", [3 * KT, P, NT], F32).ap()
        q_d = nc.dram_tensor("q_d", [H, P, NT], F32).ap()
        ya_d = nc.dram_tensor("ya_d", [KT, P, NT], F32).ap()
        yb_d = nc.dram_tensor("yb_d", [KT, P, NT], F32).ap()
        m_d = nc.dram_tensor("m_d", [KT, P, NT], F32).ap()

        w_load = [sem("w_load0"), sem("w_load1")]
        w_hi, w_split = sem("w_hi"), sem("w_split")
        prod = sem("prod")
        ev_act = sem("ev_act")
        ev_dve = sem("ev_dve")
        o_dve, o_pool = sem("o_dve"), sem("o_pool")
        par_ld, par_tr, par_ok = sem("par_ld"), sem("par_tr"), sem("par_ok")
        ones_ok, iota_ok, dist_ok = sem("ones_ok"), sem("iota_ok"), sem("dist_ok")
        x_ld = [sem(f"x_ld{i}") for i in range(3)]
        x_tr, x_eva, x_evd, xs_d = sem("x_tr"), sem("x_eva"), sem("x_evd"), sem("xs_d")
        silu_ok, ada_mm, mod_ok = sem("silu_ok"), sem("ada_mm"), sem("mod_ok")
        ada_ld = [sem(f"ada_ld{i}") for i in range(4)]
        sq_ok, sq_mm, rt_ok = sem("sq_ok"), sem("sq_mm"), sem("rt_ok")
        h_ok, h_hi, h_lo = sem("h_ok"), sem("h_hi"), sem("h_lo")
        kw_tr, kw_ev, ki_ok = sem("kw_tr"), sem("kw_ev"), sem("ki_ok")
        kc_ld, kc_tr, kc_ev = sem("kc_ld"), sem("kc_tr"), sem("kc_ev")
        cv_ld = sem("cv_ld")
        ws_ld, ws_tr, ws_eva, ws_evd, ws_ok = (sem(n) for n in ("ws_ld", "ws_tr", "ws_eva", "ws_evd", "ws_ok"))
        bs_ld = sem("bs_ld")
        sc_mm, sc_relu, sc_add = sem("sc_mm"), sem("sc_relu"), sem("sc_add")
        srch = sem("srch")
        glu_done = sem("glu_done")
        hist_ld, hist_tr, hist_ok = sem("hist_ld"), sem("hist_tr"), sem("hist_ok")
        conv_ch, conv_ok = sem("conv_ch"), sem("conv_ok")
        gate_st = [sem("gate_st0"), sem("gate_st1")]
        qk_mm, qk_rt, qk_ri, qk_ok = sem("qk_mm"), sem("qk_rt"), sem("qk_ri"), sem("qk_ok")
        kv_tr, kv_ev, k_out, q_st, out_dma = sem("kv_tr"), sem("kv_ev"), sem("k_out"), sem("q_st"), sem("out_dma")
        ln_sq, ln_mm, ln_mean, ln_var, ln_rt, ln_ok = (sem(n) for n in (
            "ln_sq", "ln_mm", "ln_mean", "ln_var", "ln_rt", "ln_ok"))
        lnc_c, lnc_n, lnc_s = sem("lnc_c"), sem("lnc_n"), sem("lnc_s")
        ya_st = [sem("ya_st0"), sem("ya_st1")]
        tail_tr, tail_ev, tl_st = sem("tail_tr"), sem("tail_ev"), sem("tl_st")
        vg_ch, vg_ok, vg_tr, vg_ev = sem("vg_ch"), sem("vg_ok"), sem("vg_tr"), sem("vg_ev")
        mix_mm, mix_ev, yb_ok, yb_st, gv_st = (sem(n) for n in ("mix_mm", "mix_ev", "yb_ok", "yb_st", "gv_st"))
        q_ld = [sem("q_ld0"), sem("q_ld1")]
        lg_mm, lg_ev, lg_mx = sem("lg_mm"), sem("lg_ev"), sem("lg_mx")
        pr_exp, rs_ok, pr_ok = sem("pr_exp"), sem("rs_ok"), sem("pr_ok")
        pt_tr, pt_eva, pt_evd, pv_mm = sem("pt_tr"), sem("pt_eva"), sem("pt_evd"), sem("pv_mm")
        o_hi, o_lo = sem("o_hi"), sem("o_lo")
        g_ld, br_ld, m_st = ([sem(f"{n}{j}") for j in range(2)] for n in ("g_ld", "br_ld", "m_st"))
        br_hi, br_lo, mp_ld, m_ok, m_hi, m_lo = (sem(n) for n in ("br_hi", "br_lo", "mp_ld", "m_ok", "m_hi", "m_lo"))
        x1_ld = sem("x1_ld")
        f_ok, f_hi, f_lo = sem("f_ok"), sem("f_hi"), sem("f_lo")
        y_tr, y_eva, y_evd = sem("y_tr"), sem("y_eva"), sem("y_evd")
        y_st = [sem("y_st0"), sem("y_st1")]

        win = w_in[0].rearrange("(k p) c -> p k c", p=P)
        v_pa, v_pb, v_pc, v_o, v_1 = (w[0].rearrange("(k p) c -> p k c", p=P) for w in (w_pa, w_pb, w_pc, w_o, w_1))
        v_2 = w_2[0].rearrange("(g k p) c -> g p k c", p=P, k=FG)
        v_ada = w_ada[0].rearrange("(k p) c -> p k c", p=P)
        x_rows = [x_prompt[0, t * P:(t + 1) * P, :] for t in range(TT)] + [x_sample[0]]

        def stage(i, n=NT, p=P):
            return st[0:p, i, 0:n]

        def chunks(ap):
            return ap.rearrange("p (c n) -> p c n", c=CH)

        def product(s, m=P):
            return acc[0:m, s, :, 0:CW]


        def pieces(s):
            edge = SEQ - 2 * CW
            return [(acc[:, s, 0:2, 0:CW], 0, 2 * CW, 0), (acc[:, s, 2:3, 0:edge], 2 * CW, SEQ, 0),
                    (acc[:, s, 2:3, edge:CW], SEQ, NT, 1)]

        def flat(ap, n):
            return ap.rearrange("p (c n) -> p c n", n=n)

        def score_of(t):
            return score[0:rows(t), SOFF[t]:SOFF[t] + WIDTH[t]]

        def dist_of(t):
            first = SEQ - P - P * (1 if t == TT else t)
            return dist[0:rows(t), first:first + WIDTH[t]]

        def bias_of(t):
            return score_of(t) if t in SOFF else dist01[:, t * P:t * P + WIDTH[t]]

        SCORES = [(t, c, min(512, WIDTH[t] - c), h) for t in STILES for c in range(0, WIDTH[t], 512)
                  for h in range(IH)]
        NSC = len(SCORES)
        ATT = [(t, n) for t in range(TT + 1) for n in range(NKV)]

        def key_tiles(t):
            if t == TT:
                return [(0, TT, P), (P, TT + 1, DEC)]
            return [(P * b, b, P) for b in range(t + 1)]

        NPT = sum(len(key_tiles(t)) for t, _ in ATT)

        block = ctx.enter_context(nc.Block())

        @block.sync
        def _(sp):
            vecs = [(g_norm1, R_GN1), (b_dw, R_BDW), (ln_c_g, R_LCG), (ln_c_b, R_LCB), (ln_v_g, R_LVG),
                    (ln_v_b, R_LVB), (g_norm2, R_GN2), (b_2, R_B2), (b_1, R_B1), (g_q, R_GQ), (g_k, R_GK)]
            for v, r in vecs:
                n = v.shape[1] // P
                sp.dma_start(st[r:r + n, 4, 0:P], v[0].rearrange("(r p) -> r p", p=P)).then_inc(par_ld, 16)
            for v, r in [(b_ada[0], 0), (c_prompt[0], MODS), (c_sample[0], MODS + KT)]:
                n = v.shape[0] // P
                sp.dma_start(st[r:r + n, 4, P:2 * P], v.rearrange("(r p) -> r p", p=P)).then_inc(par_ld, 16)
            sp.dma_start(st[0:CONV_W, 3, 0:D], w_dw[0]).then_inc(par_ld, 16)

            def load_x(t):
                if t >= 3:
                    sp.wait_ge(x_tr, 2 * (t - 3) + 2)
                sp.dma_start(stage(t % 3, D, rows(t)), x_rows[t]).then_inc(x_ld[t % 3], 16)

            for t in range(3):
                load_x(t)
            for s in range(4):
                sp.dma_start(wada[:, s], v_ada[:, :, 2 * P * s:2 * P * (s + 1)]).then_inc(ada_ld[s], 16)
            for t in range(3, TT + 1):
                load_x(t)
            with sp.Fori(1, MODS // 8) as i:
                for s in range(4):
                    sp.wait_ge(ada_mm, 4 * i + (s - 3))
                    sp.dma_start(wada[:, s], v_ada[:, :, bass.ds((4 * i + s) * 2 * P, 2 * P)]).then_inc(ada_ld[s], 16)

            def load_w(n, src, s, m=P, k=KT):
                wait(sp, w_split, n - 1)
                sp.dma_start(raw[:, s, 0:k, 0:m], src).then_inc(w_load[s], 16)

            load_w(N_KI, win[:, :, C_KI:C_KI + KIW], 0, KIW)
            load_w(N_QI, win[:, :, C_QI:C_QI + P], N_QI % 2)
            sp.wait_ge(x_eva, TT + 1)
            sp.wait_ge(x_evd, TT + 1)
            sp.wait_ge(ones_ok, 6)
            sp.dma_start(xT_d, xT[:, :, :]).then_inc(xs_d, 16)
            sp.dma_start(vtok[:, TT, :], cache_v[0, 0].rearrange("j n d -> j (n d)")).then_inc(cv_ld, 16)
            for j in range(1, 4):
                load_w(N_QI + j, win[:, :, C_QI + P * j:C_QI + P * (j + 1)], (N_QI + j) % 2)
            with sp.Fori(0, KT) as i:
                for j, col in enumerate((C_VAL, C_GATE)):
                    load_w(N_GLU + 2 * i + j, win[:, :, bass.ds(P * i + col, P)], (N_GLU + j) % 2)

            def load_run(n0, view, count, col=0):
                with sp.Fori(0, count // 2) as i:
                    for j in range(2):
                        load_w(n0 + 2 * i + j, view[:, :, bass.ds(2 * P * i + (col + P * j), P)], (n0 + j) % 2)

            load_run(N_GATE, win, 3 * KT, C_GL)
            load_run(N_KV, win, 2 * NKV, C_K)
            load_run(N_Q, win, H, C_Q)
            load_run(N_VG, win, KT, C_V)
            load_run(N_U, win, KT, C_U)
            load_run(N_PC, v_pc, KT)
            load_run(N_PB, v_pb, KT)
            load_run(N_PA, v_pa, KT)
            load_run(N_WO, v_o, KT)
            with sp.Fori(0, NG) as g:
                for j in range(FG):
                    load_w(GT * g + (N_MLP + j), v_1[:, :, bass.ds(FG * P * g + P * j, P)], (N_MLP + j) % 2)
                for j in range(KT):
                    load_w(GT * g + (N_MLP + FG + j), v_2[bass.ds(g, 1), :, :, P * j:P * (j + 1)].rearrange(
                        "a p k c -> p (a k) c"), (N_MLP + FG + j) % 2, k=FG)

            for t in range(TT + 1):
                sp.wait_ge(y_eva, t + 1)
                sp.wait_ge(y_evd, t + 1)
                dst = y_sample[0] if t == TT else y_prompt[0, P * t:P * (t + 1), :]
                sp.dma_start(dst, stage(t % 2, D, rows(t))).then_inc(y_st[t % 2], 16)
            sp.wait_ge(y_st[0], 16 * 5)
            sp.wait_ge(y_st[1], 16 * 4)

        @block.gpsimd
        def _(pool):
            own = Order(pool, o_pool)
            own.mark(nc.gpsimd.memset(ident[:, :], 0.0))
            nc.gpsimd.memset(mean_d[:, :], 1.0 / D).then_inc(ones_ok, 1)
            nc.gpsimd.memset(mean_h[:, :], 1.0 / DH).then_inc(ones_ok, 1)
            nc.gpsimd.memset(ones_row[:, :], 1.0).then_inc(ones_ok, 1)
            nc.gpsimd.memset(eps[:, :], EPS).then_inc(ones_ok, 1)
            nc.gpsimd.memset(one[:, :], 1.0)
            nc.gpsimd.memset(xT[:, :, TOK:NT], 0.0).then_inc(ones_ok, 1)
            nc.gpsimd.iota(dist[:, :], pattern=[[-1, SEQ]], base=SEQ - P, channel_multiplier=1,
                           allow_small_or_imprecise_dtypes=True).then_inc(iota_ok, 1)
            own.settle()
            nc.gpsimd.affine_select(out=ident[:, :], in_=ident[:, :], compare_op=ALU.not_equal, fill=1.0,
                                    base=0, pattern=[[-1, P]], channel_multiplier=1).then_inc(ones_ok, 1)

            def split_tile(n, count, s, m=P, k=KT):
                pool.wait_ge(w_load[s], 16 * count)
                wait(pool, prod, n - 1)
                part = raw[:, s, 0:k, 0:m]
                nc.gpsimd.tensor_tensor(whi[:, s, 0:k, 0:m], part, one[:, 0:1].unsqueeze(2).broadcast_to([P, k, m]),
                                        ALU.mult).then_inc(w_hi, 1)
                pool.wait_ge(w_hi, n + 1)
                nc.gpsimd.tensor_tensor(wlo[:, s, 0:k, 0:m], part, whi[:, s, 0:k, 0:m].bitcast(F32),
                                        ALU.subtract).then_inc(w_split, 1)

            def split_pair(n0, i, j):
                split_tile(2 * i + (n0 + j), i + ((n0 + j) // 2 + 1), (n0 + j) % 2)

            split_tile(N_KI, 1, 0, KIW)
            split_tile(N_QI, 1, 1)

            def lo_parts(x, first):
                for k in range(KT):
                    pool.wait_ge(h_hi, first + k + 1)
                    nc.gpsimd.tensor_tensor(x[:, 1, k, :], stage(1 + 3 * (k % 2)), x[:, 0, k, :].bitcast(F32),
                                            ALU.subtract).then_inc(h_lo, 1)

            lo_parts(xa, 0)
            split_tile(2, 2, 0)
            pool.wait_ge(ws_eva, 1)
            pool.wait_ge(ws_evd, 1)
            nc.gpsimd.affine_select(out=wmT[:, :, :], in_=wmT[:, :, :], compare_op=ALU.is_ge, fill=0.0,
                                    base=0, pattern=[[0, KT], [1, P]], channel_multiplier=-1).then_inc(ws_ok, 1)
            for n in range(3, N_GLU + 2):
                split_tile(n, n // 2 + 1, n % 2)

            pool.wait_ge(sc_mm, NSC)
            nc.gpsimd.memset(apad[:, :, 0:HIST], 0.0).then_inc(glu_done, 1)
            with pool.Fori(0, KT) as i:
                for j in range(2):
                    split_pair(N_GLU + 2, i, j)
                pool.wait_ge(ev_act, 2 * i + (N_GLU + 2))
                nc.gpsimd.tensor_tensor(apad[:, bass.ds(i, 1), HIST:HIST + SEQ], st[:, 2:3, 0:SEQ],
                                        st[:, 3:4, 0:SEQ], ALU.mult)
                nc.gpsimd.tensor_tensor(apad[:, bass.ds(i, 1), APW - DEC:APW], st[:, 2:3, SEQ:TOK],
                                        st[:, 3:4, SEQ:TOK], ALU.mult).then_inc(glu_done, 1)
            with pool.Fori(0, (N_PC - N_GATE) // 2) as i:
                for j in range(2):
                    split_pair(N_GATE + 2, i, j)

            for i in range((TT + 1) * H):
                t, h = divmod(i, H)
                pool.wait_ge(rs_ok, i + 1)
                part = stage(h % G, WIDTH[t], rows(t))
                nc.gpsimd.tensor_scalar(part, part, ri[0:rows(t), h:h + 1], None, ALU.mult).then_inc(pr_ok, 1)

            for b, (n0, x) in enumerate(((N_PC + 2, xb), (N_PB + 2, xa))):
                with pool.Fori(0, KT // 2) as i:
                    for j in range(2):
                        split_pair(n0, i, j)
                        pool.wait_ge(br_hi, 2 * i + (KT * b + j + 1))
                        nc.gpsimd.tensor_tensor(x[:, 1, bass.ds(2 * i + j, 1), :], st[:, 2 + j:3 + j, 0:NT],
                                                x[:, 0, bass.ds(2 * i + j, 1), :].bitcast(F32),
                                                ALU.subtract).then_inc(br_lo, 1)
            with pool.Fori(0, KT // 2) as i:
                for j in range(2):
                    split_pair(N_PA + 2, i, j)
                    pool.wait_ge(m_hi, 2 * i + (j + 1))
                    nc.gpsimd.tensor_tensor(xb[:, 1, bass.ds(2 * i + j, 1), :], st[:, 4:5, 0:NT],
                                            xb[:, 0, bass.ds(2 * i + j, 1), :].bitcast(F32),
                                            ALU.subtract).then_inc(m_lo, 1)
            with pool.Fori(0, KT // 2) as i:
                for j in range(2):
                    split_pair(N_WO + 2, i, j)
            lo_parts(xb, KT)
            pool.sem_inc(f_lo, 2)

            def hidden_group(g, last):
                for j in range(GT):
                    n = N_MLP + 2 + j
                    if not (last and j >= GT - 2):
                        split_tile(GT * g + n, (GT // 2) * g + (n // 2 + 1), n % 2,
                                   k=KT if (j + 2) % GT < FG else FG)
                    if j < FG:
                        pool.wait_ge(f_hi, FG * g + (j + 1))
                        nc.gpsimd.tensor_tensor(xf[:, 1, j, :], stage(2 + j % 2), xf[:, 0, j, :].bitcast(F32),
                                                ALU.subtract).then_inc(f_lo, 1)

            with pool.Fori(0, NG - 1) as g:
                hidden_group(g, False)
            hidden_group(NG - 1, True)

        @block.scalar
        def _(act):
            act.wait_ge(par_ok, 3)
            nc.scalar.activation(cT[:, :, :], mod_b[:, MODS:MODS + 2 * KT].rearrange("p (g k) -> p g k", g=2),
                                 ACT.Silu).then_inc(silu_ok, 1)
            act.wait_ge(iota_ok, 1)
            nc.scalar.activation(dist[:, :], dist[:, :], ACT.Abs).then_inc(dist_ok, 1)
            for t in range(TT + 1):
                act.wait_ge(x_tr, 2 * t + 1)
                r = rows(t)
                nc.scalar.activation(xT[:, 0:4, P * t:P * t + r],
                                     aux[:, 0, 0:4 * r].rearrange("p (k n) -> p k n", k=4), ACT.Copy).then_inc(x_eva, 1)

            def rms_and_hi(src, x, first):
                for k in range(KT):
                    wait(act, sq_mm, first + max(k - 1, 0))
                    nc.scalar.activation(stage(k % 2), src[:, k, :], ACT.Square).then_inc(sq_ok, 1)
                act.wait_ge(sq_mm, first + KT)
                nc.scalar.activation(chunks(stage(2)), product(1), ACT.Sqrt, bias=eps[:, 0:1]).then_inc(rt_ok, 1)
                for k in range(KT):
                    act.wait_ge(h_ok, first + k + 1)
                    nc.scalar.activation(x[:, 0, k, :], stage(1 + 3 * (k % 2)), ACT.Copy).then_inc(h_hi, 1)

            act.wait_ge(x_evd, TT + 1)
            act.wait_ge(x_eva, TT + 1)
            act.wait_ge(ones_ok, 6)
            rms_and_hi(xT, xa, 0)

            act.wait_ge(h_lo, KT)
            act.dma_start(st[:, 3, 0:D].rearrange("p (g j) -> p g j", g=KT),
                          w_s[0].rearrange("g i j -> i g j")).then_inc(ws_ld, 16)
            act.dma_start(st[:, 4, 0:IDIM], cache_kidx[0, 0]).then_inc(kc_ld, 16)
            act.dma_start(st[:, 4, IDIM:2 * IDIM], cache_kidx[0, 0]).then_inc(kc_ld, 16)
            act.dma_start(st[:, 4, P:3 * P], cache_k[0, 0].rearrange("j n d -> j (n d)")).then_inc(kc_ld, 16)
            act.dma_start(st[0:HIST, 2, 0:D], cache_conv[0, 0]).then_inc(hist_ld, 16)

            act.wait_ge(prod, N_KI + 1)
            nc.scalar.activation(chunks(stage(0, NT, KIW)), product(0, KIW), ACT.Copy).then_inc(ev_act, 1)
            act.wait_ge(ws_tr, 2)
            nc.scalar.activation(wmT[:, 4:8, :], flat(aux[:, 1, :], P), ACT.Copy).then_inc(ws_eva, 1)
            act.wait_ge(xs_d, 16)
            for j in range(IH * IDIM // P):
                act.wait_ge(prod, N_QI + j + 1)
                nc.scalar.activation(chunks(qiT[:, j, :]), product((N_QI + j) % 2), ACT.Copy).then_inc(ev_act, 1)
            act.wait_ge(kw_ev, 4)
            act.dma_start(new_ki_p[0, 0].rearrange("(t p) c -> p t c", p=P), kiwi[:, 0:TT, 0:IDIM]).then_inc(out_dma, 16)
            act.dma_start(new_ki_s[0, 0], kiwi[0:DEC, TT, 0:IDIM]).then_inc(out_dma, 16)
            act.wait_ge(kw_tr, 3)
            act.wait_ge(ki_ok, 1)
            for i, (t, c, w, h) in enumerate(SCORES):
                act.wait_ge(sc_mm, i + 1)
                wait(act, sc_add, i - 1)
                nc.scalar.activation(st[0:rows(t), i % 2, 0:w], aux[0:rows(t), i % 2, 0:w], ACT.Relu).then_inc(sc_relu, 1)

            act.wait_ge(hist_tr, 1)
            act.wait_ge(ws_tr, 2)
            with act.Fori(0, KT) as i:
                act.wait_ge(prod, 2 * i + (N_GLU + 1))
                act.wait_ge(glu_done, i + 1)
                nc.scalar.activation(chunks(stage(2)), product(N_GLU % 2), ACT.Copy).then_inc(ev_act, 1)
                act.wait_ge(prod, 2 * i + (N_GLU + 2))
                nc.scalar.activation(chunks(stage(3)), product((N_GLU + 1) % 2), ACT.Sigmoid).then_inc(ev_act, 1)

            act.wait_ge(sc_add, NSC)

            def gate_pair(i):
                for j in range(2):
                    act.wait_ge(prod, 2 * i + (N_GATE + 1 + j))
                    wait(act, gate_st[j], 16 * i)
                    nc.scalar.activation(chunks(stage(j)), product((N_GATE + j) % 2), ACT.Sigmoid).then_inc(ev_act, 1)
                    act.wait_ge(ev_act, 2 * i + (N_GATE + 1 + j))
                    act.dma_start(gate_d[bass.ds(2 * i + j, 1)].rearrange("a p n -> p (a n)"),
                                  stage(j)).then_inc(gate_st[j], 16)

            gate_pair(0)
            with act.Fori(1, 3 * KT // 2) as i:
                gate_pair(i)
            for j in range(2):
                act.wait_ge(gate_st[j], 16 * 3 * KT // 2)

            act.wait_ge(glu_done, KT + 1)

            def qk_tile(n, s, idx):
                act.wait_ge(prod, n + 1)
                wait(act, qk_ok, idx)
                nc.scalar.activation(chunks(stage(0)), product(s), ACT.Copy)
                nc.scalar.activation(chunks(stage(1)), product(s), ACT.Square).then_inc(ev_act, 1)
                for c in range(CH):
                    act.wait_ge(qk_mm, CH * idx + (c + 1))
                    nc.scalar.activation(st[:, 2, CW * c:CW * (c + 1)], aux[:, c % 2, 0:CW], ACT.Sqrt,
                                         bias=eps[:, 0:1]).then_inc(qk_rt, 1)

            for j in range(NKV):
                qk_tile(N_KV + j, (N_KV + j) % 2, j)
                act.wait_ge(kv_ev, CH * (j + 1))
                act.dma_start(new_k_p[0, 0, :, j, :].rearrange("(t p) d -> p t d", p=P),
                              st[:, 4, 0:SEQ].rearrange("p (t d) -> p t d", t=TT)).then_inc(k_out, 16)
                act.dma_start(new_k_s[0, 0, :, j, :], st[0:DEC, 4, SEQ:SEQ + DH]).then_inc(k_out, 16)
            for j in range(NKV):
                n = N_KV + NKV + j
                act.wait_ge(prod, n + 1)
                act.wait_ge(qk_ok, NKV)
                wait(act, kv_tr, CH * (NKV + j) if j else 0)
                nc.scalar.activation(chunks(stage(0)), product(n % 2), ACT.Copy).then_inc(ev_act, 1)
            act.wait_ge(kv_ev, CH * 2 * NKV)
            act.wait_ge(out_dma, 32)
            act.dma_start(bs_row[:, :, :], b_s[0:1]).then_inc(bs_ld, 16)
            act.dma_start(new_v_p[0, 0].rearrange("(t p) n d -> p t (n d)", p=P), vtok[:, 0:TT, :]).then_inc(out_dma, 16)
            act.dma_start(new_v_s[0, 0].rearrange("j n d -> j (n d)"), vtok[0:DEC, TT + 1, :]).then_inc(out_dma, 16)

            def query_pair(i):
                for j in range(2):
                    qk_tile(2 * i + (N_Q + j), (N_Q + j) % 2, 2 * i + (NKV + j))
                    act.wait_ge(qk_ok, 2 * i + (NKV + j + 1))
                    act.dma_start(q_d[bass.ds(2 * i + j, 1)].rearrange("a p n -> p (a n)"), stage(4)).then_inc(q_st, 16)

            with act.Fori(0, H // 2) as i:
                query_pair(i)

            def layer_norm_stats(src, nth):
                first = KT * nth
                for k in range(KT):
                    wait(act, ln_mm, first + max(k - 1, 0))
                    nc.scalar.activation(stage(k % 2), src[:, k, 0:NT], ACT.Square).then_inc(ln_sq, 1)
                act.wait_ge(ln_mm, first + KT)
                nc.scalar.activation(chunks(stage(2)), product(0), ACT.Copy).then_inc(ln_mean, 1)
                act.wait_ge(ln_var, nth + 1)
                nc.scalar.activation(stage(4), stage(3), ACT.Sqrt, bias=eps[:, 0:1]).then_inc(ln_rt, 1)

            act.wait_ge(conv_ok, KT)
            act.wait_ge(qk_ok, NKV + H)
            layer_norm_stats(apad, 0)

            def swish_pair(i):
                for j in range(2):
                    act.wait_ge(lnc_n, 2 * i + (j + 1))
                    nc.scalar.activation(stage(j), stage(j), ACT.Silu, bias=par[:, bass.ds(2 * i + (R_LCB + j), 1)],
                                         scale=par[:, bass.ds(2 * i + (R_LCG + j), 1)]).then_inc(lnc_s, 1)
                    act.wait_ge(lnc_s, 2 * i + (j + 1))
                    act.dma_start(ya_d[bass.ds(2 * i + j, 1)].rearrange("a p n -> p (a n)"), stage(j)).then_inc(ya_st[j], 16)

            with act.Fori(0, KT // 2) as i:
                swish_pair(i)
            act.wait_ge(tail_ev, 4)
            act.dma_start(new_conv_p[0, 0], st[0:HIST, 4, 0:D]).then_inc(tl_st, 16)
            act.dma_start(new_conv_s[0, 0], st[0:HIST, 3, 0:D]).then_inc(tl_st, 16)

            with act.Fori(0, KT // 2) as i:
                for j in range(2):
                    act.wait_ge(prod, 2 * i + (N_VG + j + 1))
                    nc.scalar.activation(zT[:, bass.ds(2 * i + j, 1), :].rearrange("p a (c n) -> p (a c) n", c=CH),
                                         product((N_VG + j) % 2), ACT.Gelu_apprx_tanh).then_inc(ev_act, 1)
            act.wait_ge(ev_act, N_U)
            act.wait_ge(ya_st[0], 16 * KT // 2)
            act.wait_ge(ya_st[1], 16 * KT // 2)
            layer_norm_stats(zT, 1)
            with act.Fori(0, KT // 2) as i:
                for j in range(2):
                    act.wait_ge(vg_ev, 6 * i + (3 * j + 3))
                    act.dma_start(new_gv_s[0, 0, :, bass.ds(2 * P * i + P * j, P)],
                                  st[0:DEC, 1, SEQ:SEQ + P]).then_inc(gv_st, 16)
                    act.wait_ge(prod, 2 * i + (N_U + j + 1))
                    act.wait_ge(vg_ok, 2 * i + (j + 1))
                    nc.scalar.activation(zT[:, bass.ds(2 * i + j, 1), :].rearrange("p a (c n) -> p (a c) n", c=CH),
                                         product((N_U + j) % 2), ACT.Gelu_apprx_tanh).then_inc(ev_act, 1)
                    for m, (a, b) in enumerate(((0, 512), (512, SEQ), (SEQ, TOK))):
                        act.wait_ge(mix_mm, 6 * i + (3 * j + m + 1))
                        if m == 0:
                            act.wait_ge(yb_ok, 2 * i + (j + 1))
                        nc.scalar.activation(st[:, 4, a:b], aux[:, (m + 1) % 2, 0:b - a], ACT.Copy).then_inc(mix_ev, 1)
                    act.wait_ge(yb_ok, 2 * i + (j + 2))
                    act.dma_start(yb_d[bass.ds(2 * i + j, 1)].rearrange("a p n -> p (a n)"),
                                  zT[:, bass.ds(2 * i + j, 1), :].rearrange("p a n -> p (a n)")).then_inc(yb_st, 16)

            act.wait_ge(q_st, 16 * H)
            act.wait_ge(out_dma, 16 * 4)
            act.wait_ge(gv_st, 16 * KT)
            act.wait_ge(yb_st, 16 * KT)

            def load_q(t):
                if t >= 2:
                    act.wait_ge(lg_mm, H * (t - 1))
                act.dma_start((qt, qt2)[t % 2][:, :, 0:rows(t)],
                              q_d[:, :, P * t:P * t + rows(t)].rearrange("h p n -> p h n")).then_inc(q_ld[t % 2], 16)

            load_q(0)
            load_q(1)
            pt = 0
            for a, (t, n) in enumerate(ATT):
                r = rows(t)
                for h in range(G * n, G * n + G):
                    i = H * t + h
                    act.wait_ge(lg_mx, i + 1)
                    part = stage(h % G, WIDTH[t], r)
                    nc.scalar.activation(part, part, ACT.Exp, bias=nmx[0:r, h:h + 1],
                                         accum_out=rs[0:r, h:h + 1]).then_inc(pr_exp, 1)
                if n == 1 and t >= 1 and t + 1 <= TT:
                    load_q(t + 1)
                for b, (_, _, kr) in enumerate(key_tiles(t)):
                    if pt % 2 == 0:
                        act.wait_ge(pt_tr, pt + 1)
                        wait(act, pv_mm, pt - 1)
                        nc.scalar.activation(st[0:kr, 4, 0:G * r], aux[0:kr, 0, 0:G * r], ACT.Copy).then_inc(pt_eva, 1)
                    pt += 1
                act.wait_ge(pv_mm, pt)
                nc.scalar.activation(xa[:, 0, G * n:G * n + G, P * t:P * t + r],
                                     acc[:, n, 2, 0:G * r].rearrange("p (h q) -> p h q", h=G), ACT.Copy).then_inc(o_hi, 1)

            def branch_pair(b, i):
                for j in range(2):
                    idx = 2 * i + (KT * b + j)
                    gate = (2, 1, 0)[b] * KT
                    if b or not isinstance(i, int) or i:
                        act.wait_ge(m_st[j], 16 * (i + KT // 2 * b) if b < 2 else 16 * KT)
                    if b == 2:
                        wait(act, m_ok, idx - (KT + 1))
                    act.dma_start(stage(j), gate_d[bass.ds(2 * i + (gate + j), 1)].rearrange("a p n -> p (a n)"))\
                       .then_inc(g_ld[j], 16)
                    if b:
                        wait(act, m_ok, idx - KT)
                        if b == 2:
                            wait(act, m_lo, 2 * i + j)
                        act.dma_start(stage(4), m_d[bass.ds(2 * i + j, 1)].rearrange("a p n -> p (a n)")).then_inc(mp_ld, 16)
                    if b < 2:
                        wait(act, br_lo, idx - 1)
                        act.dma_start(stage(2 + j), (yb_d, ya_d)[b][bass.ds(2 * i + j, 1)].rearrange("a p n -> p (a n)"))\
                           .then_inc(br_ld[j], 16)
                        act.wait_ge(br_ld[j], 16 * (i + (KT // 2 * b + 1)))
                        nc.scalar.activation((xb, xa)[b][:, 0, bass.ds(2 * i + j, 1), :], st[:, 2 + j:3 + j, 0:NT],
                                             ACT.Copy).then_inc(br_hi, 1)
                        act.wait_ge(m_ok if b else ev_dve, idx + 1 - (KT if b else 0))
                        act.dma_start(m_d[bass.ds(2 * i + j, 1)].rearrange("a p n -> p (a n)"), stage(j)).then_inc(m_st[j], 16)
                    else:
                        act.wait_ge(m_ok, idx + (1 - KT))
                        nc.scalar.activation(xb[:, 0, bass.ds(2 * i + j, 1), :], st[:, 4:5, 0:NT], ACT.Copy).then_inc(m_hi, 1)

            act.wait_ge(o_lo, len(ATT))
            for b in range(3):
                if b == 1:
                    act.wait_ge(prod, N_PB)
                if b == 2:
                    act.wait_ge(prod, N_PA)
                branch_pair(b, 0)
                with act.Fori(1, KT // 2) as i:
                    branch_pair(b, i)

            act.wait_ge(prod, N_WO)
            act.dma_start(x1T[:, :, :], xT_d).then_inc(x1_ld, 16)
            act.wait_ge(ev_dve, 4 * KT)
            rms_and_hi(x1T, xb, KT)

            with act.Fori(0, NG) as g:
                for j in range(FG):
                    act.wait_ge(prod, GT * g + (N_MLP + j + 1))
                    act.wait_ge(f_ok, FG * g + (j + 1))
                    nc.scalar.activation(chunks(stage(j % 2)), product((N_MLP + j) % 2), ACT.Relu,
                                         bias=par[:, bass.ds(FG * g + (R_B1 + j), 1)]).then_inc(ev_act, 1)
                    act.wait_ge(f_ok, FG * g + (j + 3))
                    act.wait_ge(prod, GT * g + N_MLP)
                    nc.scalar.activation(xf[:, 0, j, :], stage(2 + j % 2), ACT.Copy).then_inc(f_hi, 1)

            for t in range(TT + 1):
                act.wait_ge(y_tr, 2 * t + 1)
                if t >= 2:
                    act.wait_ge(y_st[t % 2], 16 * (t // 2))
                r = rows(t)
                nc.scalar.activation(st[0:r, t % 2, 0:512], aux[0:r, 0, :], ACT.Copy).then_inc(y_eva, 1)
            act.wait_ge(k_out, 16 * 2 * NKV)
            act.wait_ge(tl_st, 16 * 2)

        @block.vector
        def _(dve):
            own = Order(dve, o_dve)

            def step(ins):
                own.mark(ins)
                own.settle()

            own.mark(nc.vector.memset(s_acc[:, :], 0))
            own.mark(nc.vector.memset(s_bit[:, :], 1 << (BITS - 1)))
            dve.wait_ge(par_tr, 1)
            nc.vector.tensor_copy(par[:, :], aux[:, 0, 0:R_N]).then_inc(par_ok, 1)
            nc.vector.tensor_copy(mod_b[:, :], aux[:, 0, P:P + MODS + 2 * KT]).then_inc(par_ok, 1)
            nc.vector.tensor_copy(wdwT[:, :, :], aux[:, 1, 0:256].rearrange("p (k w) -> p k w", k=KT)[:, :, 0:CONV_W])\
                .then_inc(par_ok, 1)
            dve.wait_ge(par_ok, 3)
            own.mark(nc.vector.tensor_scalar(gq[:, :], par[:, R_GQ:R_GQ + 1], float(DH) ** -0.5, None, ALU.mult))
            for t in range(TT + 1):
                dve.wait_ge(x_tr, 2 * t + 2)
                r = rows(t)
                nc.vector.tensor_copy(xT[:, 4:8, P * t:P * t + r],
                                      aux[:, 1, 0:4 * r].rearrange("p (k n) -> p k n", k=4)).then_inc(x_evd, 1)
            dve.wait_ge(ada_mm, MODS // 2)
            for g in range(2):
                nc.vector.tensor_tensor(mod[:, g, :], flat(acc[:, 0, 0, 0:2 * MODS], 2)[:, :, g], mod_b[:, 0:MODS],
                                        ALU.add).then_inc(mod_ok, 1)
            dve.wait_ge(mod_ok, 2)
            for g in range(2):
                for gain, m, r in ((gain1, M_SC1, R_GN1), (gain2, M_SC2, R_GN2)):
                    own.mark(nc.vector.scalar_tensor_tensor(gain[:, g, :], mod[:, g, m:m + KT], 1.0, par[:, r:r + KT],
                                                            ALU.add, ALU.mult))
                own.mark(nc.vector.tensor_tensor(b2g[:, g, :], mod[:, g, M_G2:M_G2 + KT], par[:, R_B2:R_B2 + KT], ALU.mult))

            def normalise(src, nth, gain, shift, add_b2):
                dve.wait_ge(rt_ok, nth + 1)
                step(nc.vector.reciprocal(stage(3), stage(2)))
                for k in range(KT):
                    wait(dve, h_ok, KT * nth + k if k else 0)
                    step(nc.vector.tensor_tensor(stage(0), src[:, k, :], stage(3), ALU.mult))
                    wait(dve, h_lo, KT * nth + k - 1 if k > 1 else 0)
                    out = 1 + 3 * (k % 2)
                    for g, (a, b) in enumerate(((0, SEQ), (SEQ, NT))):
                        ins = nc.vector.tensor_scalar(st[:, out, a:b], st[:, 0, a:b], gain[:, g, k:k + 1],
                                                      mod[:, g, shift + k:shift + k + 1], ALU.mult, ALU.add)
                    ins.then_inc(h_ok, 1)
                    if add_b2:
                        for g, (a, b) in enumerate(((0, SEQ), (SEQ, NT))):
                            ins = nc.vector.tensor_scalar(src[:, k, a:b], src[:, k, a:b], b2g[:, g, k:k + 1], None, ALU.add)
                        own.mark(ins)

            own.settle()
            normalise(xT, 0, gain1, M_SH1, False)

            dve.wait_ge(ev_act, N_KI + 1)
            dve.wait_ge(xs_d, 16)
            for half in range(2):
                for dst, (a, b) in ((0, (0, SEQ)), (SEQ + PAST, (SEQ, TOK))):
                    ins = nc.vector.tensor_copy(kiT[IDIM * half:IDIM * (half + 1), dst:dst + b - a], st[0:IDIM, 0, a:b])
            own.mark(ins)
            dve.wait_ge(kw_tr, 3)
            nc.vector.tensor_copy(kiwi[:, 0:7, :], flat(aux[:, 0, 0:7 * KIW], KIW)).then_inc(kw_ev, 1)
            nc.vector.tensor_copy(kiwi[:, 7, :], aux[:, 1, 0:KIW]).then_inc(kw_ev, 1)
            nc.vector.tensor_copy(kiwi[0:DEC, 8, :], aux[0:DEC, 1, KIW:2 * KIW]).then_inc(kw_ev, 1)
            nc.vector.tensor_copy(kiT[:, SEQ:SEQ + PAST], aux[:, 1, 2 * KIW:2 * KIW + P]).then_inc(kw_ev, 1)
            dve.wait_ge(ws_tr, 1)
            nc.vector.tensor_copy(wmT[:, 0:4, :], flat(aux[:, 0, :], P)).then_inc(ws_evd, 1)
            dve.wait_ge(kc_tr, 1)
            nc.vector.tensor_copy(kT[:, :, SEQ:SEQ + PAST], flat(aux[:, 0, 0:2 * P], P)).then_inc(kc_ev, 1)
            dve.wait_ge(kw_ev, 4)
            scale = float(IDIM) ** -0.5 * float(IH) ** -0.5
            nc.vector.tensor_scalar(wi[:, 0:TT, :], kiwi[:, 0:TT, IDIM:KIW], scale, None, ALU.mult)
            nc.vector.tensor_scalar(wi[0:DEC, TT, :], kiwi[0:DEC, TT, IDIM:KIW], scale, None, ALU.mult).then_inc(ki_ok, 1)
            dve.wait_ge(ki_ok, 1)
            for i, (t, c, w, h) in enumerate(SCORES):
                dve.wait_ge(sc_relu, i + 1)
                out = score_of(t)[:, c:c + w]
                part = st[0:rows(t), i % 2, 0:w]
                if h == 0:
                    nc.vector.tensor_scalar(out, part, wi[0:rows(t), t, h:h + 1], None, ALU.mult).then_inc(sc_add, 1)
                else:
                    dve.wait_ge(sc_add, i)
                    nc.vector.scalar_tensor_tensor(out, part, wi[0:rows(t), t, h:h + 1], out, ALU.mult, ALU.add)\
                        .then_inc(sc_add, 1)
            dve.wait_ge(sc_add, NSC)
            for t in STILES[:-1]:
                ins = nc.vector.memset(score[0:CHUNK, SOFF[t] + WIDTH[t] - CHUNK:SOFF[t] + WIDTH[t]], LOW)
            own.mark(ins)
            own.mark(nc.vector.memset(s_cnt[:, :], 0.0))
            dve.wait_ge(hist_tr, 1)
            nc.vector.tensor_copy(apad[:, :, HIST + SEQ:2 * HIST + SEQ],
                                  flat(aux[:, 0, 0:256], 32)[:, :, 0:HIST]).then_inc(hist_ok, 1)
            own.settle()

            PER_BIT = NS + 4

            def step_at(done, ins):
                ins.then_inc(srch, 1)
                dve.wait_ge(srch, done + 1)

            def count(done, bar_of):
                for u, t in enumerate(STILES):
                    short = TOPK - TOPK_S if t == TT else 0
                    step_at(done + u, nc.vector.tensor_scalar(
                        st[0:rows(t), 4, 0:WIDTH[t]], score_of(t), bar_of(u, t), float(short),
                        ALU.is_ge, ALU.add, accum_out=s_cnt[0:rows(t), u:u + 1]))

            dve.wait_ge(kc_tr, 1)
            count(0, lambda u, t: 0.0)
            step_at(NS, nc.vector.tensor_scalar(s_flip[:, :], s_cnt[:, :], float(TOPK), -1.0, ALU.is_lt, ALU.mult))
            with dve.Fori(0, BITS) as i:
                done = PER_BIT * i + (NS + 1)
                step_at(done, nc.vector.scalar_tensor_tensor(s_cand[:, :], s_acc[:, :], s_bit[:, 0:1], s_flip[:, :],
                                                             ALU.bitwise_or, ALU.bitwise_xor))
                count(done + 1, lambda u, t: s_cand[0:rows(t), u:u + 1].bitcast(F32))
                step_at(done + (NS + 1), nc.vector.tensor_scalar(s_take[:, :], s_cnt[:, :], float(TOPK), -1.0,
                                                                 ALU.is_ge, ALU.mult))
                step_at(done + (NS + 2), nc.vector.scalar_tensor_tensor(
                    s_acc[:, :], s_take[:, :], s_bit[:, 0:1], s_acc[:, :], ALU.bitwise_and, ALU.bitwise_or))
                step_at(done + (NS + 3), nc.vector.tensor_scalar(s_bit[:, :], s_bit[:, :], 1, None,
                                                                 ALU.logical_shift_right))
            own.mark(nc.vector.tensor_tensor(s_cand[:, :], s_acc[:, :], s_flip[:, :], ALU.bitwise_xor))

            with dve.Fori(0, KT) as i:
                row = apad[:, bass.ds(i, 1), :].rearrange("p a n -> p (a n)")
                tap = wdwT[:, bass.ds(i, 1), :].rearrange("p a w -> p (a w)")
                conv = st[:, 4, 0:CONV_N]
                links = [0]

                def link(ins):
                    links[0] += 1
                    ins.then_inc(conv_ch, 1)
                    dve.wait_ge(conv_ch, CONV_W * i + links[0])

                dve.wait_ge(glu_done, i + 2)
                dve.wait_ge(hist_ok, 1)
                for m, a in enumerate((SEQ, APW - HIST)):
                    nc.vector.tensor_scalar(ctail[:, bass.ds(i, 1), m:m + 1, :].rearrange("p a b n -> p (a b n)"),
                                            row[:, a:a + HIST], 1.0, None, ALU.mult)
                link(nc.vector.tensor_scalar(conv, row[:, 1:1 + CONV_N], tap[:, 1:2],
                                             par[:, bass.ds(i + R_BDW, 1)], ALU.mult, ALU.add))
                for w in range(2, CONV_W):
                    link(nc.vector.scalar_tensor_tensor(conv, row[:, w:w + CONV_N], tap[:, w:w + 1], conv,
                                                        ALU.mult, ALU.add))
                link(nc.vector.scalar_tensor_tensor(conv, row[:, 0:CONV_N], tap[:, 0:1], conv, ALU.mult, ALU.add))
                nc.vector.tensor_scalar(row[:, 0:SEQ], conv[:, 0:SEQ], 1.0, None, ALU.mult)
                nc.vector.tensor_scalar(row[:, TOK:NT], conv[:, 0:NT - TOK], 0.0, None, ALU.mult)
                nc.vector.tensor_copy(row[:, SEQ:TOK], conv[:, CONV_N - DEC:CONV_N]).then_inc(conv_ok, 1)
                dve.wait_ge(conv_ok, i + 1)

            def norm_qk(idx, out_pieces, gain):
                dve.wait_ge(qk_rt, CH * idx + CH)
                nc.vector.reciprocal(stage(3), stage(2)).then_inc(qk_ri, 1)
                dve.wait_ge(qk_ri, idx + 1)
                for out, a, b in out_pieces:
                    ins = nc.vector.scalar_tensor_tensor(out, st[:, 0, a:b], gain, st[:, 3, a:b], ALU.mult, ALU.mult)
                ins.then_inc(qk_ok, 1)

            for j in range(NKV):
                norm_qk(j, [(kT[:, j, 0:SEQ], 0, SEQ), (kT[:, j, SEQ + PAST:NKEY], SEQ, TOK)], par[:, R_GK:R_GK + 1])
                if j:
                    dve.wait_ge(k_out, 16 * 2 * j)
                for m, (a, w, r) in enumerate(((0, 512, P), (512, 512, P), (SEQ, P, DEC))):
                    dve.wait_ge(kv_tr, CH * j + m + 1)
                    nc.vector.tensor_copy(st[0:r, 4, a:a + w], aux[0:r, m % 2, 0:w]).then_inc(kv_ev, 1)
            dve.wait_ge(cv_ld, 16)
            for j in range(NKV):
                for m, (a, b, r) in enumerate(((0, 4, P), (4, 8, P), (TT + 1, TT + 2, DEC))):
                    dve.wait_ge(kv_tr, CH * (NKV + j) + m + 1)
                    nc.vector.tensor_copy(vtok[0:r, a:b, DH * j:DH * (j + 1)],
                                          flat(aux[0:r, m % 2, 0:P * (b - a)], P)).then_inc(kv_ev, 1)
            dve.wait_ge(k_out, 16 * 2 * NKV)

            def query_pair(i):
                for j in range(2):
                    wait(dve, q_st, 16 * (2 * i + j))
                    norm_qk(2 * i + (NKV + j), [(stage(4), 0, NT)], gq[:, 0:1])

            query_pair(0)
            with dve.Fori(1, H // 2) as i:
                query_pair(i)
            dve.wait_ge(q_st, 16 * H)

            def layer_norm_stats(nth):
                dve.wait_ge(ln_mean, nth + 1)
                step(nc.vector.tensor_tensor(stage(3), stage(2), stage(2), ALU.mult))
                step(nc.vector.scalar_tensor_tensor(chunks(stage(3)), product(1), 1.0, chunks(stage(3)),
                                                    ALU.mult, ALU.subtract))
                nc.vector.tensor_scalar(stage(3), stage(3), 0.0, None, ALU.max).then_inc(ln_var, 1)
                dve.wait_ge(ln_rt, nth + 1)
                nc.vector.reciprocal(stage(3), stage(4)).then_inc(ln_ok, 1)
                dve.wait_ge(ln_ok, nth + 1)

            layer_norm_stats(0)

            def centre_pair(i):
                for j in range(2):
                    wait(dve, ya_st[j], 16 * i)
                    nc.vector.tensor_tensor(st[:, j:j + 1, 0:NT], apad[:, bass.ds(2 * i + j, 1), 0:NT], st[:, 2:3, 0:NT],
                                            ALU.subtract).then_inc(lnc_c, 1)
                    dve.wait_ge(lnc_c, 2 * i + (j + 1))
                    nc.vector.tensor_tensor(stage(j), stage(j), stage(3), ALU.mult).then_inc(lnc_n, 1)

            centre_pair(0)
            with dve.Fori(1, KT // 2) as i:
                centre_pair(i)
            dve.wait_ge(lnc_n, KT)
            for m in range(4):
                dve.wait_ge(tail_tr, m + 1)
                nc.vector.tensor_copy(st[0:HIST, 4 - m // 2, 512 * (m % 2):512 * (m % 2 + 1)],
                                      aux[0:HIST, m % 2, :]).then_inc(tail_ev, 1)
            dve.wait_ge(tl_st, 32)

            layer_norm_stats(1)
            own.mark(nc.vector.memset(st[:, 4, TOK:NT], 0.0))
            own.mark(nc.vector.memset(st[:, 0, NT:(TT + 1) * P], 0.0))
            own.settle()
            dve.wait_ge(ln_ok, 2)
            dve.sem_inc(yb_ok, 1)

            def mix_pair(i):
                for j in range(2):
                    row = zT[:, bass.ds(2 * i + j, 1), :].rearrange("p a n -> p (a n)")
                    wait(dve, vg_tr, 6 * i + 3 * j)
                    nc.vector.tensor_tensor(stage(0), row, stage(2), ALU.subtract).then_inc(vg_ch, 1)
                    dve.wait_ge(vg_ch, 4 * i + (2 * j + 1))
                    nc.vector.tensor_tensor(stage(0), stage(0), stage(3), ALU.mult).then_inc(vg_ch, 1)
                    dve.wait_ge(vg_ch, 4 * i + (2 * j + 2))
                    nc.vector.tensor_scalar(stage(0), stage(0), par[:, bass.ds(2 * i + (R_LVG + j), 1)],
                                            par[:, bass.ds(2 * i + (R_LVB + j), 1)], ALU.mult, ALU.add).then_inc(vg_ok, 1)
                    wait(dve, gv_st, 16 * (2 * i + j))
                    wait(dve, mix_mm, 6 * i + 3 * j)
                    for m, (a, w, r) in enumerate(((0, 512, P), (512, 512, P), (SEQ, P, P))):
                        dve.wait_ge(vg_tr, 6 * i + (3 * j + m + 1))
                        nc.vector.tensor_copy(st[0:r, 1, a:a + w], aux[0:r, m % 2, 0:w]).then_inc(vg_ev, 1)
                    dve.wait_ge(mix_ev, 6 * i + (3 * j + 3))
                    nc.vector.tensor_tensor(row, row, stage(4), ALU.mult).then_inc(yb_ok, 1)

            mix_pair(0)
            with dve.Fori(1, KT // 2) as i:
                mix_pair(i)
            dve.wait_ge(gv_st, 16 * KT)
            own.settle()

            dve.wait_ge(dist_ok, 1)
            for u, t in enumerate(STILES):
                r, w = rows(t), WIDTH[t]
                sc, bar = score_of(t), s_cand[0:r, u:u + 1].bitcast(F32)
                tie, rank, more = st[0:r, 0, 0:w], st[0:r, 1, 0:w], s_cnt[0:r, u:u + 1]
                own.mark(nc.vector.tensor_scalar(tie, sc, bar, None, ALU.is_equal))
                step(nc.vector.tensor_scalar(rank, sc, bar, 0.0, ALU.is_gt, ALU.add, accum_out=more))
                own.mark(nc.vector.tensor_scalar(more, more, -1.0, float(TOPK_S if t == TT else TOPK), ALU.mult, ALU.add))
                step(nc.vector.tensor_tensor_scan(rank, tie, tie, 0.0, ALU.add, ALU.max))
                step(nc.vector.scalar_tensor_tensor(tie, rank, more, tie, ALU.is_le, ALU.mult))
                step(nc.vector.scalar_tensor_tensor(tie, sc, bar, tie, ALU.is_gt, ALU.add))
                step(nc.vector.tensor_scalar(tie, tie, 0.5, BIG, ALU.is_lt, ALU.mult))
                step(nc.vector.tensor_tensor(sc, tie, dist_of(t), ALU.add))
            for t in range(2):
                own.mark(nc.vector.tensor_copy(dist01[:, t * P:t * P + WIDTH[t]], dist_of(t)))
            own.settle()
            for t in range(2):
                own.mark(nc.vector.memset(dist01[0:CHUNK, t * P + WIDTH[t] - CHUNK:t * P + WIDTH[t]], BIG))
            own.settle()

            dve.wait_ge(yb_st, 16 * KT)
            pt = 0
            for a, (t, n) in enumerate(ATT):
                r, w = rows(t), WIDTH[t]
                for h in range(G * n, G * n + G):
                    i = H * t + h
                    part = stage(h % G, w, r)
                    dve.wait_ge(lg_mm, i + 1)
                    wait(dve, pt_tr, pt)
                    nc.vector.scalar_tensor_tensor(part, bias_of(t), -float(2.0 ** (-8.0 * (h + 1) / H)),
                                                   acc[0:r, h % 2, :, :].rearrange("p c n -> p (c n)")[:, 0:w],
                                                   ALU.mult, ALU.add).then_inc(lg_ev, 1)
                    dve.wait_ge(lg_ev, i + 1)
                    step(nc.vector.reduce_max(mx[0:r, h:h + 1], part, AX_X))
                    nc.vector.tensor_scalar(nmx[0:r, h:h + 1], mx[0:r, h:h + 1], -1.0, None, ALU.mult).then_inc(lg_mx, 1)
                for h in range(G * n, G * n + G):
                    dve.wait_ge(pr_exp, H * t + h + 1)
                    nc.vector.reciprocal(ri[0:r, h:h + 1], rs[0:r, h:h + 1]).then_inc(rs_ok, 1)
                for b, (_, _, kr) in enumerate(key_tiles(t)):
                    if pt % 2:
                        dve.wait_ge(pt_tr, pt + 1)
                        wait(dve, pv_mm, pt - 1)
                        nc.vector.tensor_copy(st[0:kr, 4, 512:512 + G * r], aux[0:kr, 1, 0:G * r]).then_inc(pt_evd, 1)
                    pt += 1
                dve.wait_ge(o_hi, a + 1)
                cols = xa[:, :, G * n:G * n + G, P * t:P * t + r]
                nc.vector.tensor_tensor(cols[:, 1], acc[:, n, 2, 0:G * r].rearrange("p (h q) -> p h q", h=G),
                                        cols[:, 0].bitcast(F32), ALU.subtract).then_inc(o_lo, 1)

            for b in range(3):
                def gated_pair(i):
                    for j in range(2):
                        n = (N_PC, N_PB, N_PA)[b]
                        dve.wait_ge(prod, 2 * i + (n + j + 1))
                        dve.wait_ge(g_ld[j], 16 * (i + (KT // 2 * b + 1)))
                        ins = nc.vector.tensor_tensor(chunks(stage(j)), product((n + j) % 2), chunks(stage(j)), ALU.mult)
                        ins.then_inc(ev_dve, 1)
                        if b == 0:
                            continue
                        dve.wait_ge(ev_dve, 2 * i + (KT * b + j + 1))
                        dve.wait_ge(mp_ld, 16 * (2 * i + (KT * (b - 1) + j + 1)))
                        nc.vector.tensor_tensor(stage(j) if b == 1 else stage(4), stage(j), stage(4), ALU.add).then_inc(m_ok, 1)

                with dve.Fori(0, KT // 2) as i:
                    gated_pair(i)

            dve.wait_ge(x1_ld, 16)
            with dve.Fori(0, KT // 2) as i:
                for j in range(2):
                    dve.wait_ge(prod, 2 * i + (N_WO + j + 1))
                    for part, c0, c1, g in pieces((N_WO + j) % 2):
                        row = x1T[:, bass.ds(2 * i + j, 1), c0:c1].rearrange("p a (c n) -> p (a c) n", n=part.shape[2])
                        ins = nc.vector.scalar_tensor_tensor(row, part, mod[:, g, bass.ds(2 * i + (M_G1 + j), 1)], row,
                                                             ALU.mult, ALU.add)
                    ins.then_inc(ev_dve, 1)
            dve.wait_ge(ev_dve, 4 * KT)
            dve.sem_inc(f_ok, 2)
            normalise(x1T, 1, gain2, M_SH2, True)
            own.settle()

            with dve.Fori(0, NG) as g:
                for j in range(FG):
                    dve.wait_ge(ev_act, FG * g + (N_PC + j + 1))
                    dve.wait_ge(f_lo, FG * g + (j + 1))
                    nc.vector.tensor_tensor(stage(2 + j % 2), stage(j % 2), stage(j % 2), ALU.mult).then_inc(f_ok, 1)
                for j in range(KT):
                    dve.wait_ge(prod, GT * g + (N_MLP + FG + j + 1))
                    for part, c0, c1, grp in pieces((N_MLP + FG + j) % 2):
                        row = flat(x1T[:, j, c0:c1], part.shape[2])
                        ins = nc.vector.scalar_tensor_tensor(row, part, mod[:, grp, M_G2 + j:M_G2 + j + 1], row,
                                                             ALU.mult, ALU.add)
                    ins.then_inc(ev_dve, 1)
            for t in range(TT + 1):
                dve.wait_ge(y_tr, 2 * t + 2)
                if t >= 2:
                    dve.wait_ge(y_st[t % 2], 16 * (t // 2))
                r = rows(t)
                nc.vector.tensor_copy(st[0:r, t % 2, 512:D], aux[0:r, 1, :]).then_inc(y_evd, 1)

        @block.tensor
        def _(pe):
            pe.wait_ge(ones_ok, 6)
            pe.wait_ge(par_ld, 16 * 15)
            nc.tensor.transpose(aux[:, 0, 0:R_N], st[0:R_N, 4, 0:P], ident[0:R_N, 0:R_N])
            nc.tensor.transpose(aux[:, 0, P:P + MODS + 2 * KT], st[0:MODS + 2 * KT, 4, P:2 * P],
                                ident[0:MODS + 2 * KT, 0:MODS + 2 * KT])
            for k in range(KT):
                last = nc.tensor.transpose(aux[:, 1, 32 * k:32 * k + CONV_W], st[0:CONV_W, 3, P * k:P * (k + 1)],
                                           ident[0:CONV_W, 0:CONV_W])
            last.then_inc(par_tr, 1)
            pe.wait_ge(par_ok, 3)
            for t in range(TT + 1):
                r = rows(t)
                pe.wait_ge(x_ld[t % 3], 16 * (t // 3 + 1))
                for half, done in ((0, x_eva), (1, x_evd)):
                    wait(pe, done, t)
                    for k in range(4):
                        last = nc.tensor.transpose(aux[:, half, r * k:r * (k + 1)],
                                                   st[0:r, t % 3, 512 * half + P * k:512 * half + P * (k + 1)],
                                                   ident[0:r, 0:r])
                    last.then_inc(x_tr, 1)

            def square_sums(first):
                for k in range(KT):
                    pe.wait_ge(sq_ok, first + k + 1)
                    for c in range(CH):
                        last = nc.tensor.matmul(acc[:, 1, c, 0:CW], mean_d[:, :], st[:, k % 2, CW * c:CW * (c + 1)],
                                                start=(k == 0), stop=(k == KT - 1))
                    last.then_inc(sq_mm, 1)

            square_sums(0)
            pe.wait_ge(silu_ok, 1)
            with pe.Fori(0, MODS // 8) as i:
                for s in range(4):
                    pe.wait_ge(ada_ld[s], 16 * i + 16)
                    for m in range(2):
                        for k in range(KT):
                            last = nc.tensor.matmul(acc[:, 0, 0, bass.ds(16 * i + (4 * s + 2 * m), 2)],
                                                    wada[:, s, k, P * m:P * (m + 1)], cT[:, :, k],
                                                    start=(k == 0), stop=(k == KT - 1))
                    last.then_inc(ada_mm, 1)

            def gemm(n, s, x, m=P, nk=KT):
                pe.wait_ge(w_split, n + 1)
                for c in range(CH):
                    for k in range(nk):
                        for p, (w, half) in enumerate(((whi, 0), (whi, 1), (wlo, 0))):
                            last = nc.tensor.matmul(acc[0:m, s, c, 0:CW], w[:, s, k, 0:m],
                                                    x[:, half, k, CW * c:CW * (c + 1)],
                                                    start=(k == 0 and p == 0), stop=(k == nk - 1 and p == 2))
                last.then_inc(prod, 1)

            def gemm_pairs(n0, count, x, evacuated, base):
                def pair(i):
                    for j in range(2):
                        wait(pe, evacuated, 2 * i + (base + j - 1))
                        gemm(2 * i + (n0 + j), (n0 + j) % 2, x)

                if base == 0:
                    pair(0)
                with pe.Fori(int(base == 0), count // 2) as i:
                    pair(i)

            pe.wait_ge(mod_ok, 2)
            pe.wait_ge(rt_ok, 1)
            pe.wait_ge(h_lo, KT)
            gemm(N_KI, 0, xa, KIW)
            gemm(N_QI, 1, xa)
            pe.wait_ge(ev_act, N_KI + 1)
            for t in range(TT + 1):
                r = rows(t)
                last = nc.tensor.transpose(aux[0:r, t // 7, KIW * (t % 7):KIW * (t % 7 + 1)], st[0:KIW, 0, P * t:P * t + r],
                                           ident[0:KIW, 0:KIW])
                if t in (6, TT):
                    last.then_inc(kw_tr, 1)
            pe.wait_ge(kc_ld, 48)
            nc.tensor.transpose(aux[:, 1, 2 * KIW:2 * KIW + P], st[:, 4, 0:P], ident[:, :]).then_inc(kw_tr, 1)
            pe.wait_ge(kw_ev, 4)
            pe.wait_ge(ws_ld, 16)
            for half in range(2):
                for g in range(4):
                    last = nc.tensor.transpose(aux[:, half, P * g:P * (g + 1)],
                                               st[:, 3, P * (4 * half + g):P * (4 * half + g + 1)], ident[:, :])
                last.then_inc(ws_tr, 1)
            pe.wait_ge(ws_evd, 1)
            for n in range(NKV):
                last = nc.tensor.transpose(aux[:, 0, P * n:P * (n + 1)], st[:, 4, P * (n + 1):P * (n + 2)], ident[:, :])
            last.then_inc(kc_tr, 1)
            for j in range(1, IH * IDIM // P):
                pe.wait_ge(ev_act, N_QI + j - 1)
                gemm(N_QI + j, (N_QI + j) % 2, xa)
            pe.wait_ge(ev_act, N_GLU)
            pe.wait_ge(ki_ok, 1)
            pe.wait_ge(kc_ev, 1)
            pe.wait_ge(ws_eva, 1)
            for i, (t, c, w, h) in enumerate(SCORES):
                wait(pe, sc_relu, i - 1)
                half = IDIM * (h % 2)
                nc.tensor.matmul(aux[0:rows(t), i % 2, 0:w], qiT[half:half + IDIM, h // 2, P * t:P * t + rows(t)],
                                 kiT[half:half + IDIM, kcol(t) + c:kcol(t) + c + w], start=True, stop=True).then_inc(sc_mm, 1)
            pe.wait_ge(sc_relu, NSC)
            pe.wait_ge(hist_ld, 16)
            for k in range(KT):
                last = nc.tensor.transpose(aux[:, 0, 32 * k:32 * k + HIST], st[0:HIST, 2, P * k:P * (k + 1)],
                                           ident[0:HIST, 0:HIST])
            last.then_inc(hist_tr, 1)
            gemm_pairs(N_GLU, 2 * KT, xa, ev_act, N_GLU)
            gemm_pairs(N_GATE, 3 * KT, xa, ev_act, N_GATE)

            def head_means(idx):
                pe.wait_ge(ev_act, idx + (N_KV + 1) if idx_is_k(idx) else idx + (N_KV + 1 + NKV))
                for c in range(CH):
                    if c < 2:
                        wait(pe, qk_rt, CH * idx)
                    else:
                        pe.wait_ge(qk_rt, CH * idx + 1)
                    nc.tensor.matmul(aux[:, c % 2, 0:CW], mean_h[:, :], st[:, 1, CW * c:CW * (c + 1)],
                                     start=True, stop=True).then_inc(qk_mm, 1)

            def idx_is_k(idx):
                return isinstance(idx, int) and idx < NKV

            def to_tokens(src, first, done):
                for m, (tiles, bank) in enumerate(((range(0, 4), 0), (range(4, 8), 1), ((TT,), 0))):
                    if m == 2:
                        pe.wait_ge(done, first + 1)
                    for q, t in enumerate(tiles):
                        part = src(t)
                        last = nc.tensor.transpose(aux[0:part.shape[1], bank, P * q:P * (q + 1)], part, ident[:, :])
                    yield last

            pe.wait_ge(hist_ok, 1)
            for j in range(NKV):
                pe.wait_ge(ev_act, N_KV + j - 1)
                gemm(N_KV + j, (N_KV + j) % 2, xa)
                if j:
                    pe.wait_ge(kv_ev, CH * j)
                head_means(j)
                pe.wait_ge(qk_ok, j + 1)
                for last in to_tokens(lambda t: kT[:, j, P * t:P * (t + 1)] if t < TT else kT[:, j, SEQ + PAST:NKEY],
                                      CH * j, kv_ev):
                    last.then_inc(kv_tr, 1)
            for j in range(NKV):
                n = N_KV + NKV + j
                pe.wait_ge(ev_act, n - 1)
                gemm(n, n % 2, xa)
                pe.wait_ge(ev_act, n + 1)
                pe.wait_ge(kv_ev, CH * (NKV + j))
                for last in to_tokens(lambda t: st[:, 0, P * t:P * t + rows(t)], CH * (NKV + j), kv_ev):
                    last.then_inc(kv_tr, 1)
            pe.wait_ge(kv_ev, CH * 2 * NKV)
            with pe.Fori(0, H // 2) as i:
                for j in range(2):
                    pe.wait_ge(ev_act, 2 * i + (N_Q + j - 1))
                    gemm(2 * i + (N_Q + j), (N_Q + j) % 2, xa)
                    head_means(2 * i + (NKV + j))

            def layer_norm_sums(src, nth):
                for k in range(KT):
                    for c in range(CH):
                        nc.tensor.matmul(acc[:, 0, c, 0:CW], mean_d[:, :], src[:, k, CW * c:CW * (c + 1)],
                                         start=(k == 0), stop=(k == KT - 1))
                    pe.wait_ge(ln_sq, KT * nth + k + 1)
                    for c in range(CH):
                        last = nc.tensor.matmul(acc[:, 1, c, 0:CW], mean_d[:, :], st[:, k % 2, CW * c:CW * (c + 1)],
                                                start=(k == 0), stop=(k == KT - 1))
                    last.then_inc(ln_mm, 1)

            pe.wait_ge(conv_ok, KT)
            pe.wait_ge(ev_act, N_VG)
            layer_norm_sums(apad, 0)
            pe.wait_ge(qk_rt, CH * (NKV + H))
            for m in range(4):
                if m >= 2:
                    pe.wait_ge(tail_ev, m - 1)
                for k in range(4):
                    last = nc.tensor.transpose(aux[0:HIST, m % 2, P * k:P * (k + 1)], ctail[:, 4 * (m % 2) + k, m // 2, :],
                                               ident[:, :])
                last.then_inc(tail_tr, 1)
            pe.wait_ge(ln_ok, 1)
            pe.wait_ge(lnc_n, KT)
            gemm_pairs(N_VG, KT, xa, ev_act, N_VG)
            pe.wait_ge(ev_act, N_U)
            layer_norm_sums(zT, 1)
            pe.wait_ge(ln_ok, 2)
            pe.wait_ge(tail_ev, 4)
            pe.wait_ge(bs_ld, 16)
            pe.wait_ge(ws_ok, 1)

            def mix_pair(i):
                for j in range(2):
                    pe.wait_ge(ev_act, 2 * i + (N_U + j - 1))
                    gemm(2 * i + (N_U + j), (N_U + j) % 2, xa)
                    pe.wait_ge(vg_ok, 2 * i + (j + 1))
                    wait(pe, mix_ev, 6 * i + 3 * j)
                    for last in to_tokens(lambda t: st[:, 0, P * t:P * (t + 1)], 6 * i + 3 * j, vg_ev):
                        last.then_inc(vg_tr, 1)
                    g = bass.ds(2 * i + j, 1)
                    for m, tiles in enumerate((range(0, 4), range(4, 8), (TT,))):
                        bank = (m + 1) % 2
                        pe.wait_ge(vg_ev, 6 * i + (3 * j + min(m + 2, 3)))
                        if m == 2:
                            pe.wait_ge(mix_ev, 6 * i + (3 * j + 1))
                        for q, t in enumerate(tiles):
                            r = rows(t)
                            out = aux[:, bank, P * q:P * q + r]
                            nc.tensor.matmul(out, st[:, 1, P * t:P * (t + 1)], wmT[:, g, 0:r], start=True, stop=False)
                            last = nc.tensor.matmul(out, ones_row[:, :], bs_row[:, g, 0:r], start=False, stop=True)
                        last.then_inc(mix_mm, 1)

            with pe.Fori(0, KT // 2) as i:
                mix_pair(i)

            pe.wait_ge(ev_act, N_PC)
            pe.wait_ge(mix_ev, CH * KT)
            pt = 0
            for a, (t, n) in enumerate(ATT):
                r, w = rows(t), WIDTH[t]
                if n == 0:
                    pe.wait_ge(q_ld[t % 2], 16 * (t // 2 + 1))
                q = (qt, qt2)[t % 2]
                for h in range(G * n, G * n + G):
                    i = H * t + h
                    wait(pe, lg_ev, i - 1)
                    for c in range(0, w, 512):
                        last = nc.tensor.matmul(acc[0:r, h % 2, c // 512, 0:min(512, w - c)], q[:, h, 0:r],
                                                kT[:, n, kcol(t) + c:kcol(t) + min(c + 512, w)], start=True, stop=True)
                    last.then_inc(lg_mm, 1)
                kts = key_tiles(t)

                def transposes(b):
                    col, _, kr = kts[b]
                    i = pt + b
                    wait(pe, (pt_eva, pt_evd)[i % 2], i // 2)
                    for h in range(G):
                        if b == 0:
                            pe.wait_ge(pr_ok, H * t + G * n + h + 1)
                        last = nc.tensor.transpose(aux[0:kr, i % 2, r * h:r * (h + 1)], st[0:r, h, col:col + kr], ident[0:r, 0:r])
                    last.then_inc(pt_tr, 1)

                def values(b):
                    _, kt, kr = kts[b]
                    i = pt + b
                    pe.wait_ge((pt_eva, pt_evd)[i % 2], i // 2 + 1)
                    if b == 0:
                        wait(pe, o_lo, a - 1)
                    nc.tensor.matmul(acc[:, n, 2, 0:G * r], vtok[0:kr, kt, DH * n:DH * (n + 1)],
                                     st[0:kr, 4, 512 * (i % 2):512 * (i % 2) + G * r],
                                     start=(b == 0), stop=(b == len(kts) - 1)).then_inc(pv_mm, 1)

                for b in range(len(kts)):
                    transposes(b)
                    if b:
                        values(b - 1)
                values(len(kts) - 1)
                pt += len(kts)

            pe.wait_ge(o_lo, len(ATT))
            gemm_pairs(N_PC, KT, xa, ev_dve, 0)
            pe.wait_ge(br_lo, KT)
            gemm_pairs(N_PB, KT, xb, ev_dve, KT)
            pe.wait_ge(br_lo, 2 * KT)
            gemm_pairs(N_PA, KT, xa, ev_dve, 2 * KT)
            pe.wait_ge(m_lo, KT)
            gemm_pairs(N_WO, KT, xb, ev_dve, 3 * KT)
            square_sums(KT)
            pe.wait_ge(rt_ok, 2)
            pe.wait_ge(h_lo, 2 * KT)
            with pe.Fori(0, NG) as g:
                for j in range(GT):
                    if j < 2:
                        pe.wait_ge(ev_dve, KT * g + (4 * KT - 1 + j))
                    elif j < 2 + FG:
                        pe.wait_ge(ev_act, FG * g + (N_PC + j - 1))
                    else:
                        pe.wait_ge(ev_dve, KT * g + (4 * KT + j - FG - 1))
                    if j == FG:
                        pe.wait_ge(f_lo, FG * g + (FG + 2))
                    gemm(GT * g + (N_MLP + j), (N_MLP + j) % 2, xb if j < FG else xf, nk=KT if j < FG else FG)
            pe.wait_ge(ev_dve, (4 + NG) * KT)
            for t in range(TT + 1):
                r = rows(t)
                for half, done in ((0, y_eva), (1, y_evd)):
                    wait(pe, done, t)
                    for k in range(4):
                        last = nc.tensor.transpose(aux[0:r, half, P * k:P * (k + 1)], x1T[:, 4 * half + k, P * t:P * t + r],
                                                   ident[:, :])
                    last.then_inc(y_tr, 1)


_INS = ['x_prompt', 'x_sample', 'c_prompt', 'c_sample', 'cache_k', 'cache_v', 'cache_kidx', 'cache_conv',
        'w_ada', 'b_ada', 'g_norm1', 'w_in', 'w_dw', 'b_dw', 'ln_c_g', 'ln_c_b', 'w_pa', 'ln_v_g', 'ln_v_b',
        'w_s', 'b_s', 'w_pb', 'g_q', 'g_k', 'w_pc', 'w_o', 'g_norm2', 'w_1', 'b_1', 'w_2', 'b_2']
_OUTS = [(1, SEQ, D), (1, DEC, D),
         (1, 1, SEQ, NKV, DH), (1, 1, SEQ, NKV, DH), (1, 1, SEQ, IDIM), (1, 1, HIST, D),
         (1, 1, DEC, NKV, DH), (1, 1, DEC, NKV, DH), (1, 1, DEC, IDIM), (1, 1, HIST, D), (1, 1, DEC, D)]


def kernel(**inputs):
    import numpy as _np
    import concourse.bacc as _bacc
    from concourse import mybir as _mybir
    from concourse.bass_utils import run_bass_kernel_spmd as _run

    nc = _bacc.Bacc("TRN2", target_bir_lowering=False, num_devices=1)
    arrays, args = {}, []
    for name in _INS:
        a = _np.ascontiguousarray(inputs[name])
        arrays[f"in_{name}_dram"] = a
        args.append(nc.dram_tensor(f"in_{name}_dram", a.shape, _mybir.dt.from_np(a.dtype), kind="ExternalInput").ap())
    for i, shape in enumerate(_OUTS):
        args.append(nc.dram_tensor(f"out_{i}_dram", shape, _mybir.dt.float32, kind="ExternalOutput").ap())
    hybrid_stream_step(nc, *args)
    r = _run(nc, [arrays], core_ids=[0])
    return tuple(r.results[0][f"out_{i}_dram"] for i in range(len(_OUTS)))
```

```python
from contextlib import ExitStack

import concourse.bass as bass
from concourse import mybir

ALU = mybir.AluOpType
ACT = mybir.ActivationFunctionType
AX_X = mybir.AxisListType.X
F32 = mybir.dt.float32
F32R = mybir.dt.float32r
I32 = mybir.dt.int32

P = 128
D = 1024
KT = D // P
SEQ, DEC, PAST = 1024, 64, 128
TT = SEQ // P
CH = 3
CW = 364
NT = CH * CW
TOK = SEQ + DEC
CONV_W = 31
HIST = CONV_W - 1
APW = HIST + SEQ + HIST + DEC
CONV_N = APW - HIST
H, DH, NKV, G = 8, 128, 2, 4
IH, IDIM = 8, 64
CHUNK = 64
TOPK, TOPK_S = 256, 48
NKEY = SEQ + PAST + DEC
EPS = 1e-6
BIG = 1.0e30
LOW = -3.0e38
FF = 4 * D
FG = 4
NG = FF // P // FG

C_VAL, C_GATE, C_U, C_V = 0, D, 2 * D, 3 * D
C_Q = 4 * D
C_K = C_Q + H * DH
C_VV = C_K + NKV * DH
C_QI = C_VV + NKV * DH
C_KI = C_QI + IH * IDIM
KIW = IDIM + IH
C_GL = C_KI + KIW

N_KI = 0
N_QI = 1
N_KV = N_QI + IH * IDIM // P
N_Q = N_KV + 2 * NKV
N_GLU = N_Q + H
N_GATE = N_GLU + 2 * KT
N_U = N_GATE + 3 * KT
N_VG = N_U + KT
N_PC = N_VG + KT
N_PB = N_PC + KT
N_PA = N_PB + KT
N_WO = N_PA + KT
N_MLP = N_WO + KT
GT = FG + KT
N_GRP = N_MLP + 1

R_GN1, R_BDW, R_LCG, R_LCB, R_LVG, R_LVB, R_GN2, R_B2 = (KT * i for i in range(8))
R_B1 = 8 * KT
R_GQ = R_B1 + FF // P
R_GK = R_GQ + 1
R_N = R_GK + 1
M_SH1, M_SC1, M_G1, M_SH2, M_SC2, M_G2 = (KT * i for i in range(6))
MODS = 6 * KT
MOD1 = 2 * KT
ADA1 = MOD1 // 2

STILES = list(range(2, TT)) + [TT]
WIDTH = [(t + 1) * P for t in range(TT)] + [PAST + DEC]
SOFF = {}
for _t in STILES:
    SOFF[_t] = sum(WIDTH[u] for u in STILES if u < _t)
SW = sum(WIDTH[t] for t in STILES)
NS = len(STILES)
BITS = 31


def kcol(t):
    return SEQ if t == TT else 0


def rows(t):
    return DEC if t == TT else P


def wait(eng, sem, value):
    if isinstance(value, int) and value <= 0:
        return
    eng.wait_ge(sem, value)


class Order:

    def __init__(self, eng, sem):
        self.eng, self.sem, self.n = eng, sem, 0

    def mark(self, ins):
        self.n += 1
        ins.then_inc(self.sem, 1)

    def settle(self):
        self.eng.wait_ge(self.sem, self.n)


def hybrid_stream_step(nc, x_prompt, x_sample, c_prompt, c_sample, cache_k, cache_v, cache_kidx, cache_conv,
                       w_ada, b_ada, g_norm1, w_in, w_dw, b_dw, ln_c_g, ln_c_b, w_pa, ln_v_g, ln_v_b,
                       w_s, b_s, w_pb, g_q, g_k, w_pc, w_o, g_norm2, w_1, b_1, w_2, b_2,
                       y_prompt, y_sample, new_k_p, new_v_p, new_ki_p, new_conv_p,
                       new_k_s, new_v_s, new_ki_s, new_conv_s, new_gv_s):
    with ExitStack() as ctx:
        def sem(name):
            return ctx.enter_context(nc.semaphore(name))

        base = 16640
        at = [base]

        def put(name, shape, dt=F32, offset=None):
            size = 4
            for s in shape[1:]:
                size *= s
            if offset is None:
                offset = at[0]
                at[0] += (size + 31) // 32 * 32
            return nc.alloc_sbuf_tensor_at(name, shape, dt, offset=offset)

        o_xa = at[0]
        xa = put("xa", [P, 2, KT, NT], F32R)
        x1T = put("x1T", [P, KT, NT], offset=o_xa)
        xf = put("xf", [P, 2, FG, NT], F32R, offset=o_xa + 4 * KT * NT)
        wada = put("wada", [P, ADA1, KT, 2 * P], offset=o_xa)
        vgc, vgt, mixed = (put(n, [P, 2, (TT + 1) * P], offset=o_xa + 8 * m * (TT + 1) * P)
                           for m, n in enumerate(("vgc", "vgt", "mixed")))
        o_b = at[0]
        xb = put("xb", [P, 2, KT, NT], F32R)
        at[0] = o_b
        score = put("score", [P, SW])
        o_ap = at[0]
        apad = put("apad", [P, KT, APW])
        xT = put("xT", [P, KT, NT], offset=o_ap)
        qiT = put("qiT", [P, IH * IDIM // P, NT], offset=o_ap)
        kiT = put("kiT", [P, NKEY], offset=o_ap + 4 * (IH * IDIM // P) * NT)
        zT = put("zT", [P, KT, NT], offset=o_ap)
        probs1 = put("probs1", [P, G, SEQ], offset=o_ap)
        kT = put("kT", [P, NKV, NKEY])
        vtok = put("vtok", [P, TT + 2, NKV * DH])
        at[0] = max(at[0], o_b + 8 * KT * NT)
        raw = put("raw", [P, 2, KT, P])
        whi = put("whi", [P, 2, KT, P], F32R)
        wlo = put("wlo", [P, 2, KT, P], F32R)
        st = put("st", [P, 5, (TT + 1) * P])
        ident = put("ident", [P, P])
        mean_d = put("mean_d", [P, P])
        mean_h = put("mean_h", [P, P])
        o_dist = at[0]
        dist = put("dist", [P, SEQ])
        dist01 = put("dist01", [P, 3 * P])
        wmT = put("wmT", [P, KT, P])
        o_q1 = at[0]
        qt = put("qt", [P, H, P])
        qt2 = put("qt2", [P, H, P], offset=o_q1 - 4 * KT * P)
        kiwi = put("kiwi", [P, TT + 1, KIW], offset=o_q1)
        wmod = [put(f"wmod{j}", [P, KT, P], offset=o) for j, o in enumerate((o_dist, o_q1))]
        par = put("par", [P, R_N])
        mod_b = put("mod_b", [P, MODS + 2 * KT])
        cT = put("cT", [P, 2, KT])
        mod = put("mod", [P, 2, MODS])
        gain1 = put("gain1", [P, 2, KT])
        gain2 = put("gain2", [P, 2, KT])
        b2g = put("b2g", [P, 2, KT])
        wdwT = put("wdwT", [P, KT, CONV_W])
        ctail = put("ctail", [P, KT, 2, HIST])
        wi = put("wi", [P, TT + 1, IH])
        eps = put("eps", [P, 1])
        gq = put("gq", [P, 1])
        one = put("one", [P, 1])
        ones_row = put("ones_row", [1, P])
        bs_row = put("bs_row", [1, KT, P], offset=o_q1)
        s_acc = put("s_acc", [P, NS], I32)
        s_flip = put("s_flip", [P, NS], I32)
        s_bit = put("s_bit", [P, 1], I32)
        s_take = put("s_take", [P, NS], I32)
        s_cand = put("s_cand", [P, NS], I32)
        s_cnt = put("s_cnt", [P, NS])
        mx = put("mx", [P, H])
        nmx = put("nmx", [P, H])
        rs = put("rs", [P, H])
        ri = put("ri", [P, H])
        assert at[0] <= nc.sbuf_usable_end, at[0]

        acc = ctx.enter_context(nc.psum_tensor("acc", [P, 2, CH, 512], F32))
        aux = ctx.enter_context(nc.psum_tensor("aux", [P, 2, 512], F32))

        xT_d = nc.dram_tensor("xT_d", [P, KT, NT], F32).ap()
        gate_d = nc.dram_tensor("gate_d", [3 * KT, P, NT], F32).ap()
        u_d = nc.dram_tensor("u_d", [KT, P, NT], F32).ap()
        q_d = nc.dram_tensor("q_d", [H, P, NT], F32).ap()
        ya_d = nc.dram_tensor("ya_d", [KT, P, NT], F32).ap()
        yb_d = nc.dram_tensor("yb_d", [KT, P, NT], F32).ap()
        m_d = nc.dram_tensor("m_d", [KT, P, NT], F32).ap()

        w_load = [sem("w_load0"), sem("w_load1")]
        w_hi, w_split = sem("w_hi"), sem("w_split")
        prod = sem("prod")
        ev_act = sem("ev_act")
        ev_dve = sem("ev_dve")
        o_dve, o_pool = sem("o_dve"), sem("o_pool")
        par_ld, par_tr, par_ok = sem("par_ld"), sem("par_tr"), sem("par_ok")
        ones_ok, iota_ok, dist_ok = sem("ones_ok"), sem("iota_ok"), sem("dist_ok")
        x_ld = [sem(f"x_ld{i}") for i in range(3)]
        x_tr, x_eva, x_evd, xs_d = sem("x_tr"), sem("x_eva"), sem("x_evd"), sem("xs_d")
        silu_ok, ada_mm, mod_ok = sem("silu_ok"), sem("ada_mm"), sem("mod_ok")
        ada_ld = [sem(f"ada_ld{s}") for s in range(ADA1)]
        wmod_ld = [sem("wmod_ld0"), sem("wmod_ld1")]
        u_ld = [sem("u_ld0"), sem("u_ld1")]
        sq_ok, sq_mm, rt_ok = sem("sq_ok"), sem("sq_mm"), sem("rt_ok")
        sq_add = sem("sq_add")
        h_ok, h_hi, h_lo = sem("h_ok"), sem("h_hi"), sem("h_lo")
        kw_tr, kw_ev, ki_ok = sem("kw_tr"), sem("kw_ev"), sem("ki_ok")
        kc_ld, kc_tr, kc_ev = sem("kc_ld"), sem("kc_tr"), sem("kc_ev")
        cv_ld = sem("cv_ld")
        ws_ld, ws_tr, ws_eva, ws_evd, ws_ok = (sem(n) for n in ("ws_ld", "ws_tr", "ws_eva", "ws_evd", "ws_ok"))
        bs_ld = sem("bs_ld")
        sc_mm, sc_relu, sc_add = sem("sc_mm"), sem("sc_relu"), sem("sc_add")
        mask_ok = sem("mask_ok")
        srch = sem("srch")
        glu_done = sem("glu_done")
        hist_ld, hist_tr, hist_ok = sem("hist_ld"), sem("hist_tr"), sem("hist_ok")
        conv_ch, conv_ok = sem("conv_ch"), sem("conv_ok")
        gate_st = [sem("gate_st0"), sem("gate_st1")]
        qk_mm, qk_rt, qk_ri, qk_ok = sem("qk_mm"), sem("qk_rt"), sem("qk_ri"), sem("qk_ok")
        kv_tr, kv_ev, k_out, q_st, out_dma = sem("kv_tr"), sem("kv_ev"), sem("k_out"), sem("q_st"), sem("out_dma")
        ln_sq, ln_mm, ln_mean, ln_var, ln_rt, ln_ok = (sem(n) for n in (
            "ln_sq", "ln_mm", "ln_mean", "ln_var", "ln_rt", "ln_ok"))
        lnc_c, lnc_n, lnc_s = sem("lnc_c"), sem("lnc_n"), sem("lnc_s")
        ya_st = [sem("ya_st0"), sem("ya_st1")]
        tail_tr, tail_ev, tl_st = sem("tail_tr"), sem("tail_ev"), sem("tl_st")
        vg_ch, vg_ok, vg_tr, vg_ev = sem("vg_ch"), sem("vg_ok"), sem("vg_tr"), sem("vg_ev")
        mix_mm, mix_ev, yb_ok, yb_st = (sem(n) for n in ("mix_mm", "mix_ev", "yb_ok", "yb_st"))
        gv_st = [sem("gv_st0"), sem("gv_st1")]
        xa_ok = sem("xa_ok")
        v_add = sem("v_add")
        q_ld = [sem("q_ld0"), sem("q_ld1")]
        lg_mm, lg_ev, lg_mx = sem("lg_mm"), sem("lg_ev"), sem("lg_mx")
        pr_exp, rs_ok, pr_ok = sem("pr_exp"), sem("rs_ok"), sem("pr_ok")
        pt_tr, pt_eva, pt_evd, pv_mm = sem("pt_tr"), sem("pt_eva"), sem("pt_evd"), sem("pv_mm")
        o_hi, o_lo = sem("o_hi"), sem("o_lo")
        g_ld, br_ld, m_st = ([sem(f"{n}{j}") for j in range(2)] for n in ("g_ld", "br_ld", "m_st"))
        br_hi, br_lo, mp_ld, m_ok, m_hi, m_lo = (sem(n) for n in ("br_hi", "br_lo", "mp_ld", "m_ok", "m_hi", "m_lo"))
        x1_ld = sem("x1_ld")
        f_ok, f_hi, f_lo = sem("f_ok"), sem("f_hi"), sem("f_lo")
        y_tr, y_eva, y_evd = sem("y_tr"), sem("y_eva"), sem("y_evd")
        y_st = [sem("y_st0"), sem("y_st1")]

        win = w_in[0].rearrange("(k p) c -> p k c", p=P)
        v_pa, v_pb, v_pc, v_o, v_1 = (w[0].rearrange("(k p) c -> p k c", p=P) for w in (w_pa, w_pb, w_pc, w_o, w_1))
        v_2 = w_2[0].rearrange("(g k p) c -> g p k c", p=P, k=FG)
        v_ada = w_ada[0].rearrange("(k p) c -> p k c", p=P)
        x_rows = [x_prompt[0, t * P:(t + 1) * P, :] for t in range(TT)] + [x_sample[0]]

        def stage(i, n=NT, p=P):
            return st[0:p, i, 0:n]

        def chunks(ap):
            return ap.rearrange("p (c n) -> p c n", c=CH)

        def product(s, m=P):
            return acc[0:m, s, :, 0:CW]


        def pieces(s):
            edge = SEQ - 2 * CW
            return [(acc[:, s, 0:2, 0:CW], 0, 2 * CW, 0), (acc[:, s, 2:3, 0:edge], 2 * CW, SEQ, 0),
                    (acc[:, s, 2:3, edge:CW], SEQ, NT, 1)]

        def flat(ap, n):
            return ap.rearrange("p (c n) -> p c n", n=n)

        def score_of(t):
            return score[0:rows(t), SOFF[t]:SOFF[t] + WIDTH[t]]

        def dist_of(t):
            first = SEQ - P - P * (1 if t == TT else t)
            return dist[0:rows(t), first:first + WIDTH[t]]

        def bias_of(t):
            return score_of(t) if t in SOFF else dist01[:, t * P:t * P + WIDTH[t]]

        SCORES = [(t, c, min(512, WIDTH[t] - c), h) for t in STILES for c in range(0, WIDTH[t], 512)
                  for h in range(IH)]
        NSC = len(SCORES)
        ATT = [(t, n) for t in range(TT + 1) for n in range(NKV)]

        def key_tiles(t):
            if t == TT:
                return [(0, TT, P), (P, TT + 1, DEC)]
            return [(P * b, b, P) for b in range(t + 1)]


        def probs(a, h):
            t, _ = ATT[a]
            return (st if a % 2 == 0 else probs1)[0:rows(t), h, 0:WIDTH[t]]

        BLOCKS = [(a, b) for a, (t, _) in enumerate(ATT) for b in range(len(key_tiles(t)))]
        FIRST = [BLOCKS.index((a, 0)) for a in range(len(ATT))] + [len(BLOCKS)]

        def attention_steps():
            for a in range(-1, len(ATT)):
                for h in range(G):
                    n = FIRST[a + 1] - FIRST[a] if a >= 0 else 0
                    yield (a + 1 if a + 1 < len(ATT) else None), h, a, range(n * h // G, n * (h + 1) // G)

        block = ctx.enter_context(nc.Block())

        @block.sync
        def _(sp):
            vecs = [(g_norm1, R_GN1), (b_dw, R_BDW), (ln_c_g, R_LCG), (ln_c_b, R_LCB), (ln_v_g, R_LVG),
                    (ln_v_b, R_LVB), (g_norm2, R_GN2), (b_2, R_B2), (b_1, R_B1), (g_q, R_GQ), (g_k, R_GK)]
            for v, r in vecs:
                n = v.shape[1] // P
                sp.dma_start(st[r:r + n, 4, 0:P], v[0].rearrange("(r p) -> r p", p=P)).then_inc(par_ld, 16)
            for v, r in [(b_ada[0], 0), (c_prompt[0], MODS), (c_sample[0], MODS + KT)]:
                n = v.shape[0] // P
                sp.dma_start(st[r:r + n, 4, P:2 * P], v.rearrange("(r p) -> r p", p=P)).then_inc(par_ld, 16)
            sp.dma_start(st[0:CONV_W, 3, 0:D], w_dw[0]).then_inc(par_ld, 16)

            def load_x(t):
                if t >= 3:
                    sp.wait_ge(x_tr, 2 * (t - 3) + 2)
                sp.dma_start(stage(t % 3, D, rows(t)), x_rows[t]).then_inc(x_ld[t % 3], 16)

            for t in range(3):
                load_x(t)
            for s in range(ADA1):
                sp.dma_start(wada[:, s], v_ada[:, :, 2 * P * s:2 * P * (s + 1)]).then_inc(ada_ld[s], 16)
                if s < TT - 2:
                    load_x(s + 3)

            def load_w(n, src, s, m=P, k=KT):
                wait(sp, w_split, n - 1)
                sp.dma_start(raw[:, s, 0:k, 0:m], src).then_inc(w_load[s], 16)

            load_w(N_KI, win[:, :, C_KI:C_KI + KIW], 0, KIW)
            load_w(N_QI, win[:, :, C_QI:C_QI + P], N_QI % 2)
            sp.wait_ge(x_eva, TT + 1)
            sp.wait_ge(x_evd, TT + 1)
            sp.wait_ge(ones_ok, 6)
            sp.dma_start(xT_d, xT[:, :, :]).then_inc(xs_d, 16)
            sp.dma_start(vtok[:, TT, :], cache_v[0, 0].rearrange("j n d -> j (n d)")).then_inc(cv_ld, 16)
            for j in range(1, 4):
                load_w(N_QI + j, win[:, :, C_QI + P * j:C_QI + P * (j + 1)], (N_QI + j) % 2)
            def load_run(n0, view, count, col=0):
                with sp.Fori(0, count // 2) as i:
                    for j in range(2):
                        load_w(n0 + 2 * i + j, view[:, :, bass.ds(2 * P * i + (col + P * j), P)], (n0 + j) % 2)

            def load_wmod(i, j):
                if not isinstance(i, int) or i:
                    sp.wait_ge(ada_mm, 2 * i + (ADA1 + j - 1))
                sp.dma_start(wmod[j][:, :, :], v_ada[:, :, bass.ds(2 * P * i + (MOD1 + j) * P, P)]).then_inc(wmod_ld[j], 16)

            def gate_pair(i):
                for j in range(2):
                    load_w(N_GATE + 2 * i + j, win[:, :, bass.ds(2 * P * i + (C_GL + P * j), P)], (N_GATE + j) % 2)
                for j in range(2):
                    load_wmod(i, j)

            load_run(N_KV, win, 2 * NKV, C_K)
            load_run(N_Q, win, H, C_Q)
            with sp.Fori(0, KT) as i:
                for j, col in enumerate((C_VAL, C_GATE)):
                    load_w(N_GLU + 2 * i + j, win[:, :, bass.ds(P * i + col, P)], (N_GLU + j) % 2)
            sp.wait_ge(out_dma, 32)
            gate_pair(0)
            with sp.Fori(1, 3 * KT // 2) as i:
                gate_pair(i)
            with sp.Fori(0, KT // 2) as i:
                for j in range(2):
                    load_w(N_U + 2 * i + j, win[:, :, bass.ds(2 * P * i + (C_U + P * j), P)], (N_U + j) % 2)
                for j in range(2):
                    load_wmod(i + 3 * KT // 2, j)
            load_run(N_VG, win, KT, C_V)
            load_run(N_PC, v_pc, KT)
            load_run(N_PB, v_pb, KT)
            load_run(N_PA, v_pa, KT)
            load_run(N_WO, v_o, KT)
            load_w(N_MLP, v_1[:, :, 0:P], N_MLP % 2)

            def load_group(g, last):
                n = N_GRP
                for j in range(1, FG + 1 - last):
                    load_w(GT * g + n, v_1[:, :, bass.ds(FG * P * g + P * j, P)], n % 2)
                    n += 1
                for j in range(KT):
                    load_w(GT * g + n, v_2[bass.ds(g, 1), :, :, P * j:P * (j + 1)].rearrange(
                        "a p k c -> p (a k) c"), n % 2, k=FG)
                    n += 1

            with sp.Fori(0, NG - 1) as g:
                load_group(g, 0)
            load_group(NG - 1, 1)

            for t in range(TT + 1):
                sp.wait_ge(y_eva, t + 1)
                sp.wait_ge(y_evd, t + 1)
                dst = y_sample[0] if t == TT else y_prompt[0, P * t:P * (t + 1), :]
                sp.dma_start(dst, stage(t % 2, D, rows(t))).then_inc(y_st[t % 2], 16)
            sp.wait_ge(y_st[0], 16 * 5)
            sp.wait_ge(y_st[1], 16 * 4)

        @block.gpsimd
        def _(pool):
            own = Order(pool, o_pool)
            own.mark(nc.gpsimd.memset(ident[:, :], 0.0))
            nc.gpsimd.memset(mean_d[:, :], 1.0 / D).then_inc(ones_ok, 1)
            nc.gpsimd.memset(mean_h[:, :], 1.0 / DH).then_inc(ones_ok, 1)
            nc.gpsimd.memset(ones_row[:, :], 1.0).then_inc(ones_ok, 1)
            nc.gpsimd.memset(eps[:, :], EPS).then_inc(ones_ok, 1)
            nc.gpsimd.memset(one[:, :], 1.0)
            nc.gpsimd.memset(xT[:, :, TOK:NT], 0.0).then_inc(ones_ok, 1)
            own.settle()
            nc.gpsimd.affine_select(out=ident[:, :], in_=ident[:, :], compare_op=ALU.not_equal, fill=1.0,
                                    base=0, pattern=[[-1, P]], channel_multiplier=1).then_inc(ones_ok, 1)

            def split_tile(n, count, s, m=P, k=KT):
                pool.wait_ge(w_load[s], 16 * count)
                wait(pool, prod, n - 1)
                part = raw[:, s, 0:k, 0:m]
                nc.gpsimd.tensor_tensor(whi[:, s, 0:k, 0:m], part, one[:, 0:1].unsqueeze(2).broadcast_to([P, k, m]),
                                        ALU.mult).then_inc(w_hi, 1)
                pool.wait_ge(w_hi, n + 1)
                nc.gpsimd.tensor_tensor(wlo[:, s, 0:k, 0:m], part, whi[:, s, 0:k, 0:m].bitcast(F32),
                                        ALU.subtract).then_inc(w_split, 1)

            def split_pair(n0, i, j):
                split_tile(2 * i + (n0 + j), i + ((n0 + j) // 2 + 1), (n0 + j) % 2)

            split_tile(N_KI, 1, 0, KIW)
            split_tile(N_QI, 1, 1)

            def lo_parts(x, first):
                for k in range(KT):
                    pool.wait_ge(h_hi, first + k + 1)
                    nc.gpsimd.tensor_tensor(x[:, 1, k, :], stage(1 + 3 * (k % 2)), x[:, 0, k, :].bitcast(F32),
                                            ALU.subtract).then_inc(h_lo, 1)

            lo_parts(xa, 0)
            split_tile(2, 2, 0)
            pool.wait_ge(ws_eva, 1)
            pool.wait_ge(ws_evd, 1)
            nc.gpsimd.affine_select(out=wmT[:, :, :], in_=wmT[:, :, :], compare_op=ALU.is_ge, fill=0.0,
                                    base=0, pattern=[[0, KT], [1, P]], channel_multiplier=-1).then_inc(ws_ok, 1)
            with pool.Fori(0, (N_GLU - 1) // 2) as i:
                for j in range(2):
                    split_pair(3, i, j)

            pool.wait_ge(sc_mm, NSC)
            nc.gpsimd.memset(apad[:, :, 0:HIST], 0.0).then_inc(glu_done, 1)
            with pool.Fori(0, KT) as i:
                for j in range(2):
                    split_pair(N_GLU + 2, i, j)
                pool.wait_ge(ev_act, 2 * i + (N_GLU + 2))
                nc.gpsimd.tensor_tensor(apad[:, bass.ds(i, 1), HIST:HIST + SEQ], st[:, 2:3, 0:SEQ],
                                        st[:, 3:4, 0:SEQ], ALU.mult)
                nc.gpsimd.tensor_tensor(apad[:, bass.ds(i, 1), APW - DEC:APW], st[:, 2:3, SEQ:TOK],
                                        st[:, 3:4, SEQ:TOK], ALU.mult).then_inc(glu_done, 1)
            with pool.Fori(0, (N_VG - N_GATE) // 2) as i:
                for j in range(2):
                    split_pair(N_GATE + 2, i, j)
            pool.wait_ge(ada_mm, ADA1 + MODS - MOD1)
            nc.gpsimd.iota(dist[:, :], pattern=[[-1, SEQ]], base=SEQ - P, channel_multiplier=1,
                           allow_small_or_imprecise_dtypes=True).then_inc(iota_ok, 1)
            pool.wait_ge(ya_st[0], 16 * KT // 2)
            pool.wait_ge(ln_ok, 1)
            for s in (0, 4):
                nc.gpsimd.memset(stage(s), 0.0).then_inc(v_add, 1)
            with pool.Fori(0, KT // 2) as i:
                for j in range(2):
                    for m in range(2):
                        pool.wait_ge(ln_sq, 2 * i + (KT + j + 1))
                        pool.wait_ge(v_add, 4 * i + (2 * j + m + 1))
                        total = st[:, 4 * m:4 * m + 1, 0:NT]
                        part = zT[:, bass.ds(2 * i + j, 1), :] if m == 0 else st[:, 1:2, 0:NT]
                        nc.gpsimd.tensor_tensor(total, total, part, ALU.add).then_inc(v_add, 1)
                    split_pair(N_VG + 2, i, j)

            for i in range(len(ATT) * G):
                a, h = divmod(i, G)
                pool.wait_ge(rs_ok, i + 1)
                part = probs(a, h)
                nc.gpsimd.tensor_scalar(part, part, ri[0:part.shape[0], i % H:i % H + 1], None, ALU.mult).then_inc(pr_ok, 1)

            for b, (n0, x) in enumerate(((N_PC + 2, xb), (N_PB + 2, xa))):
                with pool.Fori(0, KT // 2) as i:
                    for j in range(2):
                        pool.wait_ge(br_hi, 2 * i + (KT * b + j + 1))
                        nc.gpsimd.tensor_tensor(x[:, 1, bass.ds(2 * i + j, 1), :], st[:, 2 + j:3 + j, 0:NT],
                                                x[:, 0, bass.ds(2 * i + j, 1), :].bitcast(F32),
                                                ALU.subtract).then_inc(br_lo, 1)
                        split_pair(n0, i, j)
            with pool.Fori(0, KT // 2) as i:
                for j in range(2):
                    pool.wait_ge(m_hi, 2 * i + (j + 1))
                    nc.gpsimd.tensor_tensor(xb[:, 1, bass.ds(2 * i + j, 1), :], st[:, 4:5, 0:NT],
                                            xb[:, 0, bass.ds(2 * i + j, 1), :].bitcast(F32),
                                            ALU.subtract).then_inc(m_lo, 1)
                    split_pair(N_PA + 2, i, j)
            pool.wait_ge(br_lo, 2 * KT)
            nc.gpsimd.memset(stage(2), 0.0).then_inc(sq_add, 1)
            with pool.Fori(0, KT // 2) as i:
                for j in range(2):
                    pool.wait_ge(sq_ok, 2 * i + (KT + j + 1))
                    pool.wait_ge(sq_add, 2 * i + (j + 1))
                    nc.gpsimd.tensor_tensor(stage(2), stage(2), stage(j), ALU.add).then_inc(sq_add, 1)
                    split_pair(N_WO + 2, i, j)
            lo_parts(xb, KT)
            def hidden_lo(m, j):
                pool.wait_ge(f_hi, m + 1)
                nc.gpsimd.tensor_tensor(xf[:, 1, j, :], stage(2 + j % 2), xf[:, 0, j, :].bitcast(F32),
                                        ALU.subtract).then_inc(f_lo, 1)

            def hidden_group(g, first, last):
                count = GT - last
                depth = [KT] * (FG - last) + [FG] * KT + [KT] * 2
                for j in range(count):
                    n = N_GRP + j
                    if j == 0 and first:
                        hidden_lo(0, 0)
                    if not (last and j >= count - 2):
                        split_tile(GT * g + (n + 2), (GT // 2) * g + ((n + 2) // 2 + 1), n % 2, k=depth[j + 2])
                    if j < FG - 1:
                        hidden_lo(FG * g + (j + 1), j + 1)
                if not last:
                    hidden_lo(FG * g + FG, 0)

            split_tile(N_GRP + 1, (N_GRP + 1) // 2 + 1, (N_GRP + 1) % 2)
            hidden_group(0, True, 0)
            with pool.Fori(1, NG - 1) as g:
                hidden_group(g, False, 0)
            hidden_group(NG - 1, False, 1)

        @block.scalar
        def _(act):
            act.wait_ge(par_ok, 3)
            nc.scalar.activation(cT[:, :, :], mod_b[:, MODS:MODS + 2 * KT].rearrange("p (g k) -> p g k", g=2),
                                 ACT.Silu).then_inc(silu_ok, 1)
            for t in range(TT + 1):
                act.wait_ge(x_tr, 2 * t + 1)
                r = rows(t)
                nc.scalar.activation(xT[:, 0:4, P * t:P * t + r],
                                     aux[:, 0, 0:4 * r].rearrange("p (k n) -> p k n", k=4), ACT.Copy).then_inc(x_eva, 1)

            def rms_and_hi(src, x, first):
                for k in range(KT):
                    wait(act, sq_mm, first + max(k - 1, 0))
                    nc.scalar.activation(stage(k % 2), src[:, k, :], ACT.Square).then_inc(sq_ok, 1)
                act.wait_ge(sq_mm, first + KT)
                root_and_hi(x, first)

            def root_and_hi(x, first):
                nc.scalar.activation(chunks(stage(2)), product(1), ACT.Sqrt, bias=eps[:, 0:1]).then_inc(rt_ok, 1)
                for k in range(KT):
                    act.wait_ge(h_ok, first + k + 1)
                    nc.scalar.activation(x[:, 0, k, :], stage(1 + 3 * (k % 2)), ACT.Copy).then_inc(h_hi, 1)

            act.wait_ge(x_evd, TT + 1)
            act.wait_ge(x_eva, TT + 1)
            act.wait_ge(ones_ok, 6)
            rms_and_hi(xT, xa, 0)

            act.wait_ge(h_lo, KT)
            act.dma_start(st[:, 3, 0:D].rearrange("p (g j) -> p g j", g=KT),
                          w_s[0].rearrange("g i j -> i g j")).then_inc(ws_ld, 16)
            act.dma_start(st[:, 4, 0:IDIM], cache_kidx[0, 0]).then_inc(kc_ld, 16)
            act.dma_start(st[:, 4, IDIM:2 * IDIM], cache_kidx[0, 0]).then_inc(kc_ld, 16)
            act.dma_start(st[:, 4, P:3 * P], cache_k[0, 0].rearrange("j n d -> j (n d)")).then_inc(kc_ld, 16)

            act.wait_ge(prod, N_KI + 1)
            nc.scalar.activation(chunks(stage(0, NT, KIW)), product(0, KIW), ACT.Copy).then_inc(ev_act, 1)
            act.wait_ge(ws_tr, 2)
            nc.scalar.activation(wmT[:, 4:8, :], flat(aux[:, 1, :], P), ACT.Copy).then_inc(ws_eva, 1)
            act.wait_ge(xs_d, 16)
            for j in range(IH * IDIM // P):
                act.wait_ge(prod, N_QI + j + 1)
                nc.scalar.activation(chunks(qiT[:, j, :]), product((N_QI + j) % 2), ACT.Copy).then_inc(ev_act, 1)
            act.wait_ge(kw_ev, 4)
            act.dma_start(new_ki_p[0, 0].rearrange("(t p) c -> p t c", p=P), kiwi[:, 0:TT, 0:IDIM]).then_inc(out_dma, 16)
            act.dma_start(new_ki_s[0, 0], kiwi[0:DEC, TT, 0:IDIM]).then_inc(out_dma, 16)
            act.wait_ge(kw_tr, 3)

            def qk_tile(n, s, idx):
                act.wait_ge(prod, n + 1)
                wait(act, qk_ok, idx)
                nc.scalar.activation(chunks(stage(0)), product(s), ACT.Copy)
                nc.scalar.activation(chunks(stage(1)), product(s), ACT.Square).then_inc(ev_act, 1)
                for c in range(CH):
                    act.wait_ge(qk_mm, CH * idx + (c + 1))
                    nc.scalar.activation(st[:, 2, CW * c:CW * (c + 1)], aux[:, c % 2, 0:CW], ACT.Sqrt,
                                         bias=eps[:, 0:1]).then_inc(qk_rt, 1)

            for j in range(NKV):
                qk_tile(N_KV + j, (N_KV + j) % 2, j)
                act.wait_ge(kv_ev, CH * (j + 1))
                act.dma_start(new_k_p[0, 0, :, j, :].rearrange("(t p) d -> p t d", p=P),
                              st[:, 4, 0:SEQ].rearrange("p (t d) -> p t d", t=TT)).then_inc(k_out, 16)
                act.dma_start(new_k_s[0, 0, :, j, :], st[0:DEC, 4, SEQ:SEQ + DH]).then_inc(k_out, 16)
            for j in range(NKV):
                n = N_KV + NKV + j
                act.wait_ge(prod, n + 1)
                act.wait_ge(qk_ok, NKV)
                wait(act, kv_tr, CH * (NKV + j) if j else 0)
                nc.scalar.activation(chunks(stage(0)), product(n % 2), ACT.Copy).then_inc(ev_act, 1)
            act.wait_ge(kv_ev, CH * 2 * NKV)
            act.dma_start(new_v_p[0, 0].rearrange("(t p) n d -> p t (n d)", p=P), vtok[:, 0:TT, :]).then_inc(out_dma, 16)
            act.dma_start(new_v_s[0, 0].rearrange("j n d -> j (n d)"), vtok[0:DEC, TT + 1, :]).then_inc(out_dma, 16)

            def query_pair(i):
                for j in range(2):
                    qk_tile(2 * i + (N_Q + j), (N_Q + j) % 2, 2 * i + (NKV + j))
                    act.wait_ge(qk_ok, 2 * i + (NKV + j + 1))
                    act.dma_start(q_d[bass.ds(2 * i + j, 1)].rearrange("a p n -> p (a n)"), stage(4)).then_inc(q_st, 16)

            with act.Fori(0, H // 2) as i:
                query_pair(i)

            act.wait_ge(qk_ok, NKV + H)
            act.dma_start(st[0:HIST, 2, 0:D], cache_conv[0, 0]).then_inc(hist_ld, 16)
            for i, (t, c, w, h) in enumerate(SCORES):
                act.wait_ge(sc_mm, i + 1)
                wait(act, sc_add, i - 1)
                nc.scalar.activation(st[0:rows(t), i % 2, 0:w], aux[0:rows(t), i % 2, 0:w], ACT.Relu).then_inc(sc_relu, 1)

            act.wait_ge(hist_tr, 1)
            act.wait_ge(ws_tr, 2)
            with act.Fori(0, KT) as i:
                act.wait_ge(prod, 2 * i + (N_GLU + 1))
                act.wait_ge(glu_done, i + 1)
                nc.scalar.activation(chunks(stage(2)), product(N_GLU % 2), ACT.Copy).then_inc(ev_act, 1)
                act.wait_ge(prod, 2 * i + (N_GLU + 2))
                nc.scalar.activation(chunks(stage(3)), product((N_GLU + 1) % 2), ACT.Sigmoid).then_inc(ev_act, 1)

            act.wait_ge(sc_add, NSC)

            def gate_pair(i):
                for j in range(2):
                    act.wait_ge(prod, 2 * i + (N_GATE + 1 + j))
                    wait(act, gate_st[j], 16 * i)
                    nc.scalar.activation(chunks(stage(j)), product((N_GATE + j) % 2), ACT.Sigmoid).then_inc(ev_act, 1)
                    act.wait_ge(ev_act, 2 * i + (N_GATE + 1 + j))
                    act.dma_start(gate_d[bass.ds(2 * i + j, 1)].rearrange("a p n -> p (a n)"),
                                  stage(j)).then_inc(gate_st[j], 16)

            gate_pair(0)
            with act.Fori(1, 3 * KT // 2) as i:
                gate_pair(i)

            with act.Fori(0, KT // 2) as i:
                for j in range(2):
                    act.wait_ge(prod, 2 * i + (N_U + 1 + j))
                    act.wait_ge(gate_st[j], 16 * i + 16 * 3 * KT // 2)
                    nc.scalar.activation(chunks(stage(j)), product((N_U + j) % 2), ACT.Gelu_apprx_tanh).then_inc(ev_act, 1)
                    act.wait_ge(ev_act, 2 * i + (N_U + 1 + j))
                    act.dma_start(u_d[bass.ds(2 * i + j, 1)].rearrange("a p n -> p (a n)"), stage(j)).then_inc(gate_st[j], 16)
            for j in range(2):
                act.wait_ge(gate_st[j], 16 * 4 * KT // 2)
            act.wait_ge(ada_mm, ADA1 + MODS - MOD1)
            act.dma_start(bs_row[:, :, :], b_s[0:1]).then_inc(bs_ld, 16)

            def layer_norm_stats(src, nth):
                first = KT * nth
                for k in range(KT):
                    wait(act, ln_mm, first + max(k - 1, 0))
                    nc.scalar.activation(stage(k % 2), src[:, k, 0:NT], ACT.Square).then_inc(ln_sq, 1)
                mean_and_root(nth)

            def mean_and_root(nth):
                act.wait_ge(ln_mm, KT + nth)
                if nth == 1:
                    act.wait_ge(mask_ok, 1)
                nc.scalar.activation(chunks(stage(2)), product(0), ACT.Copy).then_inc(ln_mean, 1)
                act.wait_ge(ln_var, nth + 1)
                nc.scalar.activation(stage(4), stage(3), ACT.Sqrt, bias=eps[:, 0:1]).then_inc(ln_rt, 1)

            act.wait_ge(conv_ok, KT)
            act.wait_ge(tail_ev, 4)
            act.dma_start(new_conv_p[0, 0], st[0:HIST, 4, 0:D]).then_inc(tl_st, 16)
            act.dma_start(new_conv_s[0, 0], st[0:HIST, 3, 0:D]).then_inc(tl_st, 16)
            layer_norm_stats(apad, 0)
            act.wait_ge(iota_ok, 1)
            nc.scalar.activation(dist[:, :], dist[:, :], ACT.Abs).then_inc(dist_ok, 1)

            def swish_pair(i):
                for j in range(2):
                    act.wait_ge(lnc_n, 2 * i + (j + 1))
                    nc.scalar.activation(stage(j), stage(j), ACT.Silu, bias=par[:, bass.ds(2 * i + (R_LCB + j), 1)],
                                         scale=par[:, bass.ds(2 * i + (R_LCG + j), 1)]).then_inc(lnc_s, 1)
                    act.wait_ge(lnc_s, 2 * i + (j + 1))
                    act.dma_start(ya_d[bass.ds(2 * i + j, 1)].rearrange("a p n -> p (a n)"), stage(j)).then_inc(ya_st[j], 16)

            with act.Fori(0, KT // 2) as i:
                swish_pair(i)
            act.wait_ge(ya_st[1], 16 * KT // 2)
            for k in range(KT):
                act.wait_ge(prod, N_VG + k + 1)
                nc.scalar.activation(chunks(zT[:, k, :]), product((N_VG + k) % 2), ACT.Gelu_apprx_tanh).then_inc(ev_act, 1)
                act.wait_ge(ev_act, N_VG + k + 1)
                act.wait_ge(v_add, 2 * k + 2)
                nc.scalar.activation(stage(1), zT[:, k, :], ACT.Square).then_inc(ln_sq, 1)
            mean_and_root(1)

            def load_u(i, j):
                act.wait_ge(vg_ok, 2 * i + (j + 1))
                act.dma_start(zT[:, bass.ds(2 * i + j, 1), :].rearrange("p a n -> p (a n)"),
                              u_d[bass.ds(2 * i + j, 1)].rearrange("a p n -> p (a n)")).then_inc(u_ld[j % 2], 16)

            def store_gv(i, j):
                act.wait_ge(vg_ev, 6 * i + (3 * j + 3))
                act.dma_start(new_gv_s[0, 0, :, bass.ds(2 * P * i + P * j, P)],
                              vgt[0:DEC, j % 2, SEQ:SEQ + P]).then_inc(gv_st[j % 2], 16)

            def store_yb(i, j):
                wait(act, yb_ok, 2 * i + (j + 1))
                act.dma_start(yb_d[bass.ds(2 * i + j, 1)].rearrange("a p n -> p (a n)"),
                              zT[:, bass.ds(2 * i + j, 1), :].rearrange("p a n -> p (a n)")).then_inc(yb_st, 16)

            def mix_pair(i, first=False, last=False):
                for j in range(2):
                    if not (first and j == 0):
                        store_yb(i, j - 1)
                    if not (last and j):
                        load_u(i, j + 1)
                        store_gv(i, j + 1)
                    for m, (a, b) in enumerate(((0, 512), (512, SEQ), (SEQ, TOK))):
                        act.wait_ge(mix_mm, 6 * i + (3 * j + m + 1))
                        if m == 0:
                            wait(act, yb_ok, 2 * i + (j - 1))
                        nc.scalar.activation(mixed[:, j, a:b], acc[:, j, m, 0:b - a], ACT.Copy).then_inc(mix_ev, 1)

            load_u(0, 0)
            store_gv(0, 0)
            mix_pair(0, first=True)
            with act.Fori(1, KT // 2 - 1) as i:
                mix_pair(i)
            mix_pair(KT // 2 - 1, last=True)
            store_yb(KT // 2 - 1, 1)

            act.wait_ge(q_st, 16 * H)
            act.wait_ge(out_dma, 16 * 4)
            for j in range(2):
                act.wait_ge(gv_st[j], 16 * KT // 2)
            act.wait_ge(yb_st, 16 * KT)

            def load_q(t):
                if t >= 2:
                    act.wait_ge(lg_mm, H * (t - 1))
                act.dma_start((qt, qt2)[t % 2][:, :, 0:rows(t)],
                              q_d[:, :, P * t:P * t + rows(t)].rearrange("h p n -> p h n")).then_inc(q_ld[t % 2], 16)

            load_q(0)
            load_q(1)

            def attended(a):
                t, n = ATT[a]
                r = rows(t)
                act.wait_ge(pv_mm, FIRST[a + 1])
                nc.scalar.activation(xa[:, 0, G * n:G * n + G, P * t:P * t + r],
                                     acc[:, n, 2, 0:G * r].rearrange("p (h q) -> p h q", h=G), ACT.Copy).then_inc(o_hi, 1)

            for nxt, h, a, blocks in attention_steps():
                for b in blocks:
                    i = FIRST[a] + b
                    if i % 2 == 0:
                        t, n = ATT[a]
                        r, kr = rows(t), key_tiles(t)[b][2]
                        act.wait_ge(pt_tr, i + 1)
                        wait(act, pv_mm, i - 1)
                        nc.scalar.activation(st[0:kr, 4, 0:G * r], aux[0:kr, 0, 0:G * r], ACT.Copy).then_inc(pt_eva, 1)
                if h == 0 and a >= 1:
                    attended(a - 1)
                if nxt is not None:
                    i = G * nxt + h
                    act.wait_ge(lg_mx, i + 1)
                    part = probs(nxt, h)
                    r = part.shape[0]
                    nc.scalar.activation(part, part, ACT.Exp, bias=nmx[0:r, i % H:i % H + 1],
                                         accum_out=rs[0:r, i % H:i % H + 1]).then_inc(pr_exp, 1)
                    t, n = ATT[nxt]
                    if h == 0 and n == 0 and 1 <= t < TT:
                        load_q(t + 1)
            attended(len(ATT) - 1)

            def branch_pair(b, i):
                for j in range(2):
                    idx = 2 * i + (KT * b + j)
                    gate = (2, 1, 0)[b] * KT
                    if b or not isinstance(i, int) or i:
                        act.wait_ge(m_st[j], 16 * (i + KT // 2 * b) if b < 2 else 16 * KT)
                    if b == 2:
                        wait(act, m_ok, idx - (KT + 1))
                    act.dma_start(stage(j), gate_d[bass.ds(2 * i + (gate + j), 1)].rearrange("a p n -> p (a n)"))\
                       .then_inc(g_ld[j], 16)
                    if b:
                        wait(act, m_ok, idx - KT)
                        if b == 2:
                            wait(act, m_lo, 2 * i + j)
                        act.dma_start(stage(4), m_d[bass.ds(2 * i + j, 1)].rearrange("a p n -> p (a n)")).then_inc(mp_ld, 16)
                    if b < 2:
                        wait(act, br_lo, idx - 1)
                        act.dma_start(stage(2 + j), (yb_d, ya_d)[b][bass.ds(2 * i + j, 1)].rearrange("a p n -> p (a n)"))\
                           .then_inc(br_ld[j], 16)
                        act.wait_ge(br_ld[j], 16 * (i + (KT // 2 * b + 1)))
                        nc.scalar.activation((xb, xa)[b][:, 0, bass.ds(2 * i + j, 1), :], st[:, 2 + j:3 + j, 0:NT],
                                             ACT.Copy).then_inc(br_hi, 1)
                        act.wait_ge(m_ok if b else ev_dve, idx + 1 - (KT if b else 0))
                        act.dma_start(m_d[bass.ds(2 * i + j, 1)].rearrange("a p n -> p (a n)"), stage(j)).then_inc(m_st[j], 16)
                    else:
                        act.wait_ge(m_ok, idx + (1 - KT))
                        nc.scalar.activation(xb[:, 0, bass.ds(2 * i + j, 1), :], st[:, 4:5, 0:NT], ACT.Copy).then_inc(m_hi, 1)

            act.wait_ge(o_lo, len(ATT))
            for b in range(3):
                if b == 1:
                    act.wait_ge(prod, N_PB)
                if b == 2:
                    act.wait_ge(prod, N_PA)
                branch_pair(b, 0)
                with act.Fori(1, KT // 2) as i:
                    branch_pair(b, i)

            act.wait_ge(prod, N_WO)
            act.dma_start(x1T[:, :, :], xT_d).then_inc(x1_ld, 16)
            with act.Fori(0, KT // 2) as i:
                for j in range(2):
                    act.wait_ge(ev_dve, 2 * i + (3 * KT + j + 1))
                    act.wait_ge(sq_add, 2 * i + (j + 1))
                    nc.scalar.activation(st[:, j:j + 1, 0:NT], x1T[:, bass.ds(2 * i + j, 1), :], ACT.Square).then_inc(sq_ok, 1)
            act.wait_ge(sq_mm, KT + 1)
            root_and_hi(xb, KT)

            def relu(m, n, j, bias):
                act.wait_ge(prod, n + 1)
                wait(act, f_ok, m - 1)
                nc.scalar.activation(chunks(stage(j % 2)), product((N_MLP + j) % 2), ACT.Relu, bias=bias).then_inc(ev_act, 1)

            def hidden_hi(m, j):
                act.wait_ge(f_ok, m + 1)
                nc.scalar.activation(xf[:, 0, j, :], stage(2 + j % 2), ACT.Copy).then_inc(f_hi, 1)

            relu(0, N_MLP, 0, par[:, R_B1:R_B1 + 1])
            hidden_hi(0, 0)

            def hidden_group(g, last):
                for j in range(1, FG + 1 - last):
                    relu(FG * g + j, GT * g + (N_GRP + j - 1), j % FG, par[:, bass.ds(FG * g + (R_B1 + j), 1)])
                    if j < FG:
                        hidden_hi(FG * g + j, j)
                if not last:
                    act.wait_ge(prod, GT * g + (N_GRP + GT))
                    hidden_hi(FG * g + FG, 0)

            with act.Fori(0, NG - 1) as g:
                hidden_group(g, 0)
            hidden_group(NG - 1, 1)

            for t in range(TT + 1):
                act.wait_ge(y_tr, 2 * t + 1)
                if t >= 2:
                    act.wait_ge(y_st[t % 2], 16 * (t // 2))
                r = rows(t)
                nc.scalar.activation(st[0:r, t % 2, 0:512], aux[0:r, 0, :], ACT.Copy).then_inc(y_eva, 1)
            act.wait_ge(k_out, 16 * 2 * NKV)
            act.wait_ge(tl_st, 16 * 2)

        @block.vector
        def _(dve):
            own = Order(dve, o_dve)

            def step(ins):
                own.mark(ins)
                own.settle()

            own.mark(nc.vector.memset(s_acc[:, :], 0))
            own.mark(nc.vector.memset(s_bit[:, :], 1 << (BITS - 1)))
            dve.wait_ge(par_tr, 1)
            nc.vector.tensor_copy(par[:, :], aux[:, 0, 0:R_N]).then_inc(par_ok, 1)
            nc.vector.tensor_copy(mod_b[:, :], aux[:, 0, P:P + MODS + 2 * KT]).then_inc(par_ok, 1)
            nc.vector.tensor_copy(wdwT[:, :, :], aux[:, 1, 0:256].rearrange("p (k w) -> p k w", k=KT)[:, :, 0:CONV_W])\
                .then_inc(par_ok, 1)
            dve.wait_ge(par_ok, 3)
            own.mark(nc.vector.tensor_scalar(gq[:, :], par[:, R_GQ:R_GQ + 1], float(DH) ** -0.5, None, ALU.mult))
            for t in range(TT + 1):
                dve.wait_ge(x_tr, 2 * t + 2)
                r = rows(t)
                nc.vector.tensor_copy(xT[:, 4:8, P * t:P * t + r],
                                      aux[:, 1, 0:4 * r].rearrange("p (k n) -> p k n", k=4)).then_inc(x_evd, 1)
            def modulation(psum, a, b, done, gain, m, r):
                for g in range(2):
                    nc.vector.tensor_tensor(mod[:, g, a:b], flat(psum, 2)[:, :, g], mod_b[:, a:b], ALU.add).then_inc(mod_ok, 1)
                dve.wait_ge(mod_ok, done)
                for g in range(2):
                    own.mark(nc.vector.scalar_tensor_tensor(gain[:, g, :], mod[:, g, m:m + KT], 1.0, par[:, r:r + KT],
                                                            ALU.add, ALU.mult))

            dve.wait_ge(ada_mm, ADA1)
            modulation(acc[:, 0, 0, 0:2 * MOD1], 0, MOD1, 2, gain1, M_SC1, R_GN1)

            def normalise(src, nth, gain, shift, add_b2):
                dve.wait_ge(rt_ok, nth + 1)
                step(nc.vector.reciprocal(stage(3), stage(2)))
                for k in range(KT):
                    wait(dve, h_ok, KT * nth + k if k else 0)
                    step(nc.vector.tensor_tensor(stage(0), src[:, k, :], stage(3), ALU.mult))
                    wait(dve, h_lo, KT * nth + k - 1 if k > 1 else 0)
                    out = 1 + 3 * (k % 2)
                    for g, (a, b) in enumerate(((0, SEQ), (SEQ, NT))):
                        ins = nc.vector.tensor_scalar(st[:, out, a:b], st[:, 0, a:b], gain[:, g, k:k + 1],
                                                      mod[:, g, shift + k:shift + k + 1], ALU.mult, ALU.add)
                    ins.then_inc(h_ok, 1)
                    if add_b2:
                        for g, (a, b) in enumerate(((0, SEQ), (SEQ, NT))):
                            ins = nc.vector.tensor_scalar(src[:, k, a:b], src[:, k, a:b], b2g[:, g, k:k + 1], None, ALU.add)
                        own.mark(ins)

            own.settle()
            normalise(xT, 0, gain1, M_SH1, False)

            dve.wait_ge(ev_act, N_KI + 1)
            dve.wait_ge(xs_d, 16)
            for half in range(2):
                for dst, (a, b) in ((0, (0, SEQ)), (SEQ + PAST, (SEQ, TOK))):
                    ins = nc.vector.tensor_copy(kiT[IDIM * half:IDIM * (half + 1), dst:dst + b - a], st[0:IDIM, 0, a:b])
            own.mark(ins)
            dve.wait_ge(kw_tr, 3)
            nc.vector.tensor_copy(kiwi[:, 0:7, :], flat(aux[:, 0, 0:7 * KIW], KIW)).then_inc(kw_ev, 1)
            nc.vector.tensor_copy(kiwi[:, 7, :], aux[:, 1, 0:KIW]).then_inc(kw_ev, 1)
            nc.vector.tensor_copy(kiwi[0:DEC, 8, :], aux[0:DEC, 1, KIW:2 * KIW]).then_inc(kw_ev, 1)
            nc.vector.tensor_copy(kiT[:, SEQ:SEQ + PAST], aux[:, 1, 2 * KIW:2 * KIW + P]).then_inc(kw_ev, 1)
            dve.wait_ge(ws_tr, 1)
            nc.vector.tensor_copy(wmT[:, 0:4, :], flat(aux[:, 0, :], P)).then_inc(ws_evd, 1)
            dve.wait_ge(kc_tr, 1)
            nc.vector.tensor_copy(kT[:, :, SEQ:SEQ + PAST], flat(aux[:, 0, 0:2 * P], P)).then_inc(kc_ev, 1)
            dve.wait_ge(kw_ev, 4)
            scale = float(IDIM) ** -0.5 * float(IH) ** -0.5
            nc.vector.tensor_scalar(wi[:, 0:TT, :], kiwi[:, 0:TT, IDIM:KIW], scale, None, ALU.mult)
            nc.vector.tensor_scalar(wi[0:DEC, TT, :], kiwi[0:DEC, TT, IDIM:KIW], scale, None, ALU.mult).then_inc(ki_ok, 1)
            dve.wait_ge(ws_tr, 2)

            def norm_qk(idx, out_pieces, gain):
                dve.wait_ge(qk_rt, CH * idx + CH)
                nc.vector.reciprocal(stage(3), stage(2)).then_inc(qk_ri, 1)
                dve.wait_ge(qk_ri, idx + 1)
                for out, a, b in out_pieces:
                    ins = nc.vector.scalar_tensor_tensor(out, st[:, 0, a:b], gain, st[:, 3, a:b], ALU.mult, ALU.mult)
                ins.then_inc(qk_ok, 1)

            for j in range(NKV):
                norm_qk(j, [(kT[:, j, 0:SEQ], 0, SEQ), (kT[:, j, SEQ + PAST:NKEY], SEQ, TOK)], par[:, R_GK:R_GK + 1])
                if j:
                    dve.wait_ge(k_out, 16 * 2 * j)
                for m, (a, w, r) in enumerate(((0, 512, P), (512, 512, P), (SEQ, P, DEC))):
                    dve.wait_ge(kv_tr, CH * j + m + 1)
                    nc.vector.tensor_copy(st[0:r, 4, a:a + w], aux[0:r, m % 2, 0:w]).then_inc(kv_ev, 1)
            dve.wait_ge(cv_ld, 16)
            for j in range(NKV):
                for m, (a, b, r) in enumerate(((0, 4, P), (4, 8, P), (TT + 1, TT + 2, DEC))):
                    dve.wait_ge(kv_tr, CH * (NKV + j) + m + 1)
                    nc.vector.tensor_copy(vtok[0:r, a:b, DH * j:DH * (j + 1)],
                                          flat(aux[0:r, m % 2, 0:P * (b - a)], P)).then_inc(kv_ev, 1)
            dve.wait_ge(k_out, 16 * 2 * NKV)

            def query_pair(i):
                for j in range(2):
                    wait(dve, q_st, 16 * (2 * i + j))
                    norm_qk(2 * i + (NKV + j), [(stage(4), 0, NT)], gq[:, 0:1])

            query_pair(0)
            with dve.Fori(1, H // 2) as i:
                query_pair(i)
            dve.wait_ge(q_st, 16 * H)

            dve.wait_ge(ki_ok, 1)
            for i, (t, c, w, h) in enumerate(SCORES):
                dve.wait_ge(sc_relu, i + 1)
                out = score_of(t)[:, c:c + w]
                part = st[0:rows(t), i % 2, 0:w]
                if h == 0:
                    nc.vector.tensor_scalar(out, part, wi[0:rows(t), t, h:h + 1], None, ALU.mult).then_inc(sc_add, 1)
                else:
                    dve.wait_ge(sc_add, i)
                    nc.vector.scalar_tensor_tensor(out, part, wi[0:rows(t), t, h:h + 1], out, ALU.mult, ALU.add)\
                        .then_inc(sc_add, 1)
            dve.wait_ge(sc_add, NSC)
            for t in STILES[:-1]:
                ins = nc.vector.memset(score[0:CHUNK, SOFF[t] + WIDTH[t] - CHUNK:SOFF[t] + WIDTH[t]], LOW)
            own.mark(ins)
            own.mark(nc.vector.memset(s_cnt[:, :], 0.0))
            dve.wait_ge(hist_tr, 1)
            nc.vector.tensor_copy(apad[:, :, HIST + SEQ:2 * HIST + SEQ],
                                  flat(aux[:, 0, 0:256], 32)[:, :, 0:HIST]).then_inc(hist_ok, 1)
            own.settle()

            PER_BIT = NS + 4

            def step_at(done, ins):
                ins.then_inc(srch, 1)
                dve.wait_ge(srch, done + 1)

            SIDES = [(7, 0), (6, 0), (TT, 960), (5, 0), (2, 768), (4, 0), (3, 640)]

            def count(done, bar_of):
                for m, (t, first) in enumerate(SIDES):
                    u = STILES.index(t)
                    short = TOPK - TOPK_S if t == TT else 0
                    if m > 1:
                        dve.wait_ge(srch, done + m - 1)
                    elif m == 1:
                        dve.wait_ge(srch, done + 1)
                    nc.vector.tensor_scalar(
                        st[0:rows(t), 4, first:first + WIDTH[t]], score_of(t), bar_of(u, t), float(short),
                        ALU.is_ge, ALU.add, accum_out=s_cnt[0:rows(t), u:u + 1]).then_inc(srch, 1)
                dve.wait_ge(srch, done + NS)

            dve.wait_ge(kc_tr, 1)
            count(0, lambda u, t: 0.0)
            step_at(NS, nc.vector.tensor_scalar(s_flip[:, :], s_cnt[:, :], float(TOPK), -1.0, ALU.is_lt, ALU.mult))
            with dve.Fori(0, BITS) as i:
                done = PER_BIT * i + (NS + 1)
                step_at(done, nc.vector.scalar_tensor_tensor(s_cand[:, :], s_acc[:, :], s_bit[:, 0:1], s_flip[:, :],
                                                             ALU.bitwise_or, ALU.bitwise_xor))
                count(done + 1, lambda u, t: s_cand[0:rows(t), u:u + 1].bitcast(F32))
                step_at(done + (NS + 1), nc.vector.tensor_scalar(s_take[:, :], s_cnt[:, :], float(TOPK), -1.0,
                                                                 ALU.is_ge, ALU.mult))
                step_at(done + (NS + 2), nc.vector.scalar_tensor_tensor(
                    s_acc[:, :], s_take[:, :], s_bit[:, 0:1], s_acc[:, :], ALU.bitwise_and, ALU.bitwise_or))
                step_at(done + (NS + 3), nc.vector.tensor_scalar(s_bit[:, :], s_bit[:, :], 1, None,
                                                                 ALU.logical_shift_right))
            own.mark(nc.vector.tensor_tensor(s_cand[:, :], s_acc[:, :], s_flip[:, :], ALU.bitwise_xor))

            with dve.Fori(0, KT) as i:
                row = apad[:, bass.ds(i, 1), :].rearrange("p a n -> p (a n)")
                tap = wdwT[:, bass.ds(i, 1), :].rearrange("p a w -> p (a w)")
                conv = st[:, 4, 0:CONV_N]
                halves = ((0, CONV_N // 2), (CONV_N // 2, CONV_N))

                dve.wait_ge(glu_done, i + 2)
                dve.wait_ge(hist_ok, 1)
                for m, a in enumerate((SEQ, APW - HIST)):
                    nc.vector.tensor_scalar(ctail[:, bass.ds(i, 1), m:m + 1, :].rearrange("p a b n -> p (a b n)"),
                                            row[:, a:a + HIST], 1.0, None, ALU.mult)
                for a, b in halves:
                    nc.vector.tensor_scalar(conv[:, a:b], row[:, 1 + a:1 + b], tap[:, 1:2], par[:, bass.ds(i + R_BDW, 1)],
                                            ALU.mult, ALU.add).then_inc(conv_ch, 1)
                for m, w in enumerate(list(range(2, CONV_W)) + [0]):
                    for c, (a, b) in enumerate(halves):
                        dve.wait_ge(conv_ch, 2 * CONV_W * i + (2 * m + c + 1))
                        nc.vector.scalar_tensor_tensor(conv[:, a:b], row[:, w + a:w + b], tap[:, w:w + 1], conv[:, a:b],
                                                       ALU.mult, ALU.add).then_inc(conv_ch, 1)
                dve.wait_ge(conv_ch, 2 * CONV_W * i + 2 * CONV_W)
                nc.vector.tensor_scalar(row[:, 0:SEQ], conv[:, 0:SEQ], 1.0, None, ALU.mult)
                nc.vector.tensor_scalar(row[:, TOK:NT], conv[:, 0:NT - TOK], 0.0, None, ALU.mult)
                nc.vector.tensor_copy(row[:, SEQ:TOK], conv[:, CONV_N - DEC:CONV_N]).then_inc(conv_ok, 1)
                dve.wait_ge(conv_ok, i + 1)

            dve.wait_ge(ada_mm, ADA1 + MODS - MOD1)
            modulation(aux[:, 0, 0:2 * (MODS - MOD1)], MOD1, MODS, 4, gain2, M_SC2, R_GN2)
            for g in range(2):
                own.mark(nc.vector.tensor_tensor(b2g[:, g, :], mod[:, g, M_G2:M_G2 + KT], par[:, R_B2:R_B2 + KT], ALU.mult))

            def layer_norm_stats(nth):
                dve.wait_ge(ln_mean, nth + 1)
                step(nc.vector.tensor_tensor(stage(3), stage(2), stage(2), ALU.mult))
                step(nc.vector.scalar_tensor_tensor(chunks(stage(3)), product(1), 1.0, chunks(stage(3)),
                                                    ALU.mult, ALU.subtract))
                nc.vector.tensor_scalar(stage(3), stage(3), 0.0, None, ALU.max).then_inc(ln_var, 1)
                dve.wait_ge(ln_rt, nth + 1)
                nc.vector.reciprocal(stage(3), stage(4)).then_inc(ln_ok, 1)
                dve.wait_ge(ln_ok, nth + 1)

            for m in range(4):
                dve.wait_ge(tail_tr, m + 1)
                nc.vector.tensor_copy(st[0:HIST, 4 - m // 2, 512 * (m % 2):512 * (m % 2 + 1)],
                                      aux[0:HIST, m % 2, :]).then_inc(tail_ev, 1)
            dve.wait_ge(tl_st, 32)
            layer_norm_stats(0)

            def centre_pair(i):
                for j in range(2):
                    wait(dve, ya_st[j], 16 * i)
                    nc.vector.tensor_tensor(st[:, j:j + 1, 0:NT], apad[:, bass.ds(2 * i + j, 1), 0:NT], st[:, 2:3, 0:NT],
                                            ALU.subtract).then_inc(lnc_c, 1)
                    dve.wait_ge(lnc_c, 2 * i + (j + 1))
                    nc.vector.tensor_tensor(stage(j), stage(j), stage(3), ALU.mult).then_inc(lnc_n, 1)

            centre_pair(0)
            with dve.Fori(1, KT // 2) as i:
                centre_pair(i)
            dve.wait_ge(lnc_n, KT)
            dve.wait_ge(dist_ok, 1)
            for u, t in enumerate(STILES):
                r, w = rows(t), WIDTH[t]
                sc, bar = score_of(t), s_cand[0:r, u:u + 1].bitcast(F32)
                tie, rank, more = st[0:r, 2, 0:w], st[0:r, 3, 0:w], s_cnt[0:r, u:u + 1]
                own.mark(nc.vector.tensor_scalar(tie, sc, bar, None, ALU.is_equal))
                step(nc.vector.tensor_scalar(rank, sc, bar, 0.0, ALU.is_gt, ALU.add, accum_out=more))
                own.mark(nc.vector.tensor_scalar(more, more, -1.0, float(TOPK_S if t == TT else TOPK), ALU.mult, ALU.add))
                step(nc.vector.tensor_tensor_scan(rank, tie, tie, 0.0, ALU.add, ALU.max))
                step(nc.vector.scalar_tensor_tensor(tie, rank, more, tie, ALU.is_le, ALU.mult))
                step(nc.vector.scalar_tensor_tensor(tie, sc, bar, tie, ALU.is_gt, ALU.add))
                step(nc.vector.tensor_scalar(tie, tie, 0.5, BIG, ALU.is_lt, ALU.mult))
                step(nc.vector.tensor_tensor(sc, tie, dist_of(t), ALU.add))
            for t in range(2):
                own.mark(nc.vector.tensor_copy(dist01[:, t * P:t * P + WIDTH[t]], dist_of(t)))
            own.settle()
            for t in range(2):
                own.mark(nc.vector.memset(dist01[0:CHUNK, t * P + WIDTH[t] - CHUNK:t * P + WIDTH[t]], BIG))
            own.settle()
            dve.sem_inc(mask_ok, 1)

            layer_norm_stats(1)
            for j in range(2):
                own.mark(nc.vector.memset(mixed[:, j, TOK:NT], 0.0))
                own.mark(nc.vector.memset(vgc[:, j, NT:(TT + 1) * P], 0.0))
            own.settle()

            def normalised(i, j):
                row = zT[:, bass.ds(2 * i + j, 1), :].rearrange("p a n -> p (a n)")
                out = vgc[:, j % 2, 0:NT]
                wait(dve, vg_tr, 6 * i + 3 * (j - 1))
                nc.vector.tensor_tensor(out, row, stage(2), ALU.subtract).then_inc(vg_ch, 1)
                dve.wait_ge(vg_ch, 4 * i + (2 * j + 1))
                nc.vector.tensor_tensor(out, out, stage(3), ALU.mult).then_inc(vg_ch, 1)
                dve.wait_ge(vg_ch, 4 * i + (2 * j + 2))
                nc.vector.tensor_scalar(out, out, par[:, bass.ds(2 * i + (R_LVG + j), 1)],
                                        par[:, bass.ds(2 * i + (R_LVB + j), 1)], ALU.mult, ALU.add).then_inc(vg_ok, 1)

            def by_token(i, j):
                wait(dve, gv_st[j % 2], 16 * (i + j // 2))
                wait(dve, mix_mm, 6 * i + 3 * (j - 1))
                for m, (a, w) in enumerate(((0, 512), (512, 512), (SEQ, P))):
                    dve.wait_ge(vg_tr, 6 * i + (3 * j + m + 1))
                    nc.vector.tensor_copy(vgt[:, j % 2, a:a + w], aux[:, m % 2, 0:w]).then_inc(vg_ev, 1)

            def mix_pair(i, last=False):
                for j in range(2):
                    row = zT[:, bass.ds(2 * i + j, 1), :].rearrange("p a n -> p (a n)")
                    if not last:
                        normalised(i, j + 2)
                    if not (last and j):
                        by_token(i, j + 1)
                    dve.wait_ge(mix_ev, 6 * i + (3 * j + 3))
                    dve.wait_ge(u_ld[j], 16 * (i + 1))
                    nc.vector.tensor_tensor(row, row, mixed[:, j, 0:NT], ALU.mult).then_inc(yb_ok, 1)

            normalised(0, 0)
            normalised(0, 1)
            by_token(0, 0)
            mix_pair(0)
            with dve.Fori(1, KT // 2 - 1) as i:
                mix_pair(i)
            mix_pair(KT // 2 - 1, last=True)
            for j in range(2):
                dve.wait_ge(gv_st[j], 16 * KT // 2)
            dve.wait_ge(yb_ok, KT)
            for half in range(2):
                nc.vector.tensor_scalar(xa[:, half, :, TOK:NT], one[:, 0:1].unsqueeze(2).broadcast_to([P, KT, NT - TOK]),
                                        0.0, None, ALU.mult).then_inc(xa_ok, 1)

            dve.wait_ge(yb_st, 16 * KT)

            def one_over_sum(i):
                r = rows(i // H)
                dve.wait_ge(pr_exp, i + 1)
                nc.vector.reciprocal(ri[0:r, i % H:i % H + 1], rs[0:r, i % H:i % H + 1]).then_inc(rs_ok, 1)

            def attended(a):
                t, n = ATT[a]
                r = rows(t)
                dve.wait_ge(o_hi, a + 1)
                cols = xa[:, :, G * n:G * n + G, P * t:P * t + r]
                nc.vector.tensor_tensor(cols[:, 1], acc[:, n, 2, 0:G * r].rearrange("p (h q) -> p h q", h=G),
                                        cols[:, 0].bitcast(F32), ALU.subtract).then_inc(o_lo, 1)

            for nxt, h, a, blocks in attention_steps():
                if nxt is not None:
                    i = G * nxt + h
                    t, n = ATT[nxt]
                    part = probs(nxt, h)
                    r, w = rows(t), WIDTH[t]
                    dve.wait_ge(lg_mm, i + 1)
                    if nxt >= 2:
                        dve.wait_ge(pt_tr, FIRST[nxt - 1])
                    nc.vector.scalar_tensor_tensor(part, bias_of(t), -float(2.0 ** (-8.0 * (i % H + 1) / H)),
                                                   acc[0:r, h % 2, :, :].rearrange("p c n -> p (c n)")[:, 0:w],
                                                   ALU.mult, ALU.add).then_inc(lg_ev, 1)
                    dve.wait_ge(lg_ev, i + 1)
                    step(nc.vector.reduce_max(mx[0:r, i % H:i % H + 1], part, AX_X))
                    nc.vector.tensor_scalar(nmx[0:r, i % H:i % H + 1], mx[0:r, i % H:i % H + 1], -1.0, None, ALU.mult)\
                        .then_inc(lg_mx, 1)
                if h == 0 and a >= 1:
                    attended(a - 1)
                for b in blocks:
                    j = FIRST[a] + b
                    if j % 2:
                        ta, _ = ATT[a]
                        ra, kr = rows(ta), key_tiles(ta)[b][2]
                        dve.wait_ge(pt_tr, j + 1)
                        wait(dve, pv_mm, j - 1)
                        nc.vector.tensor_copy(st[0:kr, 4, 512:512 + G * ra], aux[0:kr, 1, 0:G * ra]).then_inc(pt_evd, 1)
                if nxt is not None:
                    if h:
                        one_over_sum(i - 1)
                    if h == G - 1:
                        one_over_sum(i)
            attended(len(ATT) - 1)

            for b in range(3):
                def gated_pair(i):
                    for j in range(2):
                        n = (N_PC, N_PB, N_PA)[b]
                        dve.wait_ge(prod, 2 * i + (n + j + 1))
                        dve.wait_ge(g_ld[j], 16 * (i + (KT // 2 * b + 1)))
                        ins = nc.vector.tensor_tensor(chunks(stage(j)), product((n + j) % 2), chunks(stage(j)), ALU.mult)
                        ins.then_inc(ev_dve, 1)
                        if b == 0:
                            continue
                        dve.wait_ge(ev_dve, 2 * i + (KT * b + j + 1))
                        dve.wait_ge(mp_ld, 16 * (2 * i + (KT * (b - 1) + j + 1)))
                        nc.vector.tensor_tensor(stage(j) if b == 1 else stage(4), stage(j), stage(4), ALU.add).then_inc(m_ok, 1)

                with dve.Fori(0, KT // 2) as i:
                    gated_pair(i)

            dve.wait_ge(x1_ld, 16)
            with dve.Fori(0, KT // 2) as i:
                for j in range(2):
                    dve.wait_ge(prod, 2 * i + (N_WO + j + 1))
                    for part, c0, c1, g in pieces((N_WO + j) % 2):
                        row = x1T[:, bass.ds(2 * i + j, 1), c0:c1].rearrange("p a (c n) -> p (a c) n", n=part.shape[2])
                        ins = nc.vector.scalar_tensor_tensor(row, part, mod[:, g, bass.ds(2 * i + (M_G1 + j), 1)], row,
                                                             ALU.mult, ALU.add)
                    ins.then_inc(ev_dve, 1)
            dve.wait_ge(ev_dve, 4 * KT)
            normalise(x1T, 1, gain2, M_SH2, True)
            own.settle()

            def square(m, j):
                dve.wait_ge(ev_act, m + (N_PC + 1))
                wait(dve, f_lo, m - 1)
                nc.vector.tensor_tensor(stage(2 + j % 2), stage(j % 2), stage(j % 2), ALU.mult).then_inc(f_ok, 1)

            square(0, 0)

            def hidden_group(g, last):
                for j in range(1, FG + 1 - last):
                    square(FG * g + j, j % FG)
                for j in range(KT):
                    n = N_GRP + FG - last + j
                    dve.wait_ge(prod, GT * g + (n + 1))
                    for part, c0, c1, grp in pieces(n % 2):
                        row = flat(x1T[:, j, c0:c1], part.shape[2])
                        ins = nc.vector.scalar_tensor_tensor(row, part, mod[:, grp, M_G2 + j:M_G2 + j + 1], row,
                                                             ALU.mult, ALU.add)
                    ins.then_inc(ev_dve, 1)

            with dve.Fori(0, NG - 1) as g:
                hidden_group(g, 0)
            hidden_group(NG - 1, 1)
            for t in range(TT + 1):
                dve.wait_ge(y_tr, 2 * t + 2)
                if t >= 2:
                    dve.wait_ge(y_st[t % 2], 16 * (t // 2))
                r = rows(t)
                nc.vector.tensor_copy(st[0:r, t % 2, 512:D], aux[0:r, 1, :]).then_inc(y_evd, 1)

        @block.tensor
        def _(pe):
            pe.wait_ge(ones_ok, 6)
            pe.wait_ge(par_ld, 16 * 15)
            nc.tensor.transpose(aux[:, 0, 0:R_N], st[0:R_N, 4, 0:P], ident[0:R_N, 0:R_N])
            nc.tensor.transpose(aux[:, 0, P:P + MODS + 2 * KT], st[0:MODS + 2 * KT, 4, P:2 * P],
                                ident[0:MODS + 2 * KT, 0:MODS + 2 * KT])
            for k in range(KT):
                last = nc.tensor.transpose(aux[:, 1, 32 * k:32 * k + CONV_W], st[0:CONV_W, 3, P * k:P * (k + 1)],
                                           ident[0:CONV_W, 0:CONV_W])
            last.then_inc(par_tr, 1)
            pe.wait_ge(par_ok, 3)
            for t in range(TT + 1):
                r = rows(t)
                pe.wait_ge(x_ld[t % 3], 16 * (t // 3 + 1))
                for half, done in ((0, x_eva), (1, x_evd)):
                    wait(pe, done, t)
                    for k in range(4):
                        last = nc.tensor.transpose(aux[:, half, r * k:r * (k + 1)],
                                                   st[0:r, t % 3, 512 * half + P * k:512 * half + P * (k + 1)],
                                                   ident[0:r, 0:r])
                    last.then_inc(x_tr, 1)

            def square_sums(first):
                for k in range(KT):
                    pe.wait_ge(sq_ok, first + k + 1)
                    for c in range(CH):
                        last = nc.tensor.matmul(acc[:, 1, c, 0:CW], mean_d[:, :], st[:, k % 2, CW * c:CW * (c + 1)],
                                                start=(k == 0), stop=(k == KT - 1))
                    last.then_inc(sq_mm, 1)

            square_sums(0)
            pe.wait_ge(silu_ok, 1)
            for s in range(ADA1):
                pe.wait_ge(ada_ld[s], 16)
                for m in range(2):
                    for k in range(KT):
                        last = nc.tensor.matmul(acc[:, 0, 0, 4 * s + 2 * m:4 * s + 2 * m + 2],
                                                wada[:, s, k, P * m:P * (m + 1)], cT[:, :, k],
                                                start=(k == 0), stop=(k == KT - 1))
                last.then_inc(ada_mm, 1)

            def gemm(n, s, x, m=P, nk=KT):
                pe.wait_ge(w_split, n + 1)
                for c in range(CH):
                    for k in range(nk):
                        for p, (w, half) in enumerate(((whi, 0), (whi, 1), (wlo, 0))):
                            last = nc.tensor.matmul(acc[0:m, s, c, 0:CW], w[:, s, k, 0:m],
                                                    x[:, half, k, CW * c:CW * (c + 1)],
                                                    start=(k == 0 and p == 0), stop=(k == nk - 1 and p == 2))
                last.then_inc(prod, 1)

            def gemm_as_ready(n, s, x, ready, base, m=P):
                pe.wait_ge(w_split, n + 1)
                for k in range(KT):
                    pe.wait_ge(ready, base + k + 1)
                    for c in range(CH):
                        for p, (w, half) in enumerate(((whi, 0), (whi, 1), (wlo, 0))):
                            last = nc.tensor.matmul(acc[0:m, s, c, 0:CW], w[:, s, k, 0:m],
                                                    x[:, half, k, CW * c:CW * (c + 1)],
                                                    start=(k == 0 and p == 0), stop=(k == KT - 1 and p == 2))
                last.then_inc(prod, 1)

            def modulate(i, j):
                pe.wait_ge(wmod_ld[j], 16 * i + 16)
                for k in range(KT):
                    last = nc.tensor.matmul(aux[:, 0, bass.ds(4 * i + 2 * j, 2)], wmod[j][:, k, :], cT[:, :, k],
                                            start=(k == 0), stop=(k == KT - 1))
                last.then_inc(ada_mm, 1)

            def gemm_pairs(n0, count, x, evacuated, base, ready=None, ready_base=0):
                def pair(i):
                    for j in range(2):
                        wait(pe, evacuated, 2 * i + (base + j - 1))
                        if ready is not None and isinstance(i, int) and j == 0:
                            gemm_as_ready(n0, n0 % 2, x, ready, ready_base)
                        else:
                            gemm(2 * i + (n0 + j), (n0 + j) % 2, x)

                peeled = base == 0 or ready is not None
                if peeled:
                    pair(0)
                with pe.Fori(int(peeled), count // 2) as i:
                    pair(i)

            pe.wait_ge(mod_ok, 2)
            pe.wait_ge(rt_ok, 1)
            gemm_as_ready(N_KI, 0, xa, h_lo, 0, KIW)
            gemm(N_QI, 1, xa)
            pe.wait_ge(ev_act, N_KI + 1)
            for t in range(TT + 1):
                r = rows(t)
                last = nc.tensor.transpose(aux[0:r, t // 7, KIW * (t % 7):KIW * (t % 7 + 1)], st[0:KIW, 0, P * t:P * t + r],
                                           ident[0:KIW, 0:KIW])
                if t in (6, TT):
                    last.then_inc(kw_tr, 1)
            pe.wait_ge(kc_ld, 48)
            nc.tensor.transpose(aux[:, 1, 2 * KIW:2 * KIW + P], st[:, 4, 0:P], ident[:, :]).then_inc(kw_tr, 1)
            pe.wait_ge(kw_ev, 4)
            pe.wait_ge(ws_ld, 16)
            for half in range(2):
                for g in range(4):
                    last = nc.tensor.transpose(aux[:, half, P * g:P * (g + 1)],
                                               st[:, 3, P * (4 * half + g):P * (4 * half + g + 1)], ident[:, :])
                last.then_inc(ws_tr, 1)
            pe.wait_ge(ws_evd, 1)
            for n in range(NKV):
                last = nc.tensor.transpose(aux[:, 0, P * n:P * (n + 1)], st[:, 4, P * (n + 1):P * (n + 2)], ident[:, :])
            last.then_inc(kc_tr, 1)
            for j in range(1, IH * IDIM // P):
                pe.wait_ge(ev_act, N_QI + j - 1)
                gemm(N_QI + j, (N_QI + j) % 2, xa)
            def head_means(idx):
                pe.wait_ge(ev_act, idx + (N_KV + 1) if idx_is_k(idx) else idx + (N_KV + 1 + NKV))
                for c in range(CH):
                    if c < 2:
                        wait(pe, qk_rt, CH * idx)
                    else:
                        pe.wait_ge(qk_rt, CH * idx + 1)
                    nc.tensor.matmul(aux[:, c % 2, 0:CW], mean_h[:, :], st[:, 1, CW * c:CW * (c + 1)],
                                     start=True, stop=True).then_inc(qk_mm, 1)

            def idx_is_k(idx):
                return isinstance(idx, int) and idx < NKV

            def to_tokens(src, first, done):
                for m, (tiles, bank) in enumerate(((range(0, 4), 0), (range(4, 8), 1), ((TT,), 0))):
                    if m == 2:
                        pe.wait_ge(done, first + 1)
                    for q, t in enumerate(tiles):
                        part = src(t)
                        last = nc.tensor.transpose(aux[0:part.shape[1], bank, P * q:P * (q + 1)], part, ident[:, :])
                    yield last

            pe.wait_ge(kc_ev, 1)
            pe.wait_ge(ws_eva, 1)
            for j in range(NKV):
                pe.wait_ge(ev_act, N_KV + j - 1)
                gemm(N_KV + j, (N_KV + j) % 2, xa)
                if j:
                    pe.wait_ge(kv_ev, CH * j)
                head_means(j)
                pe.wait_ge(qk_ok, j + 1)
                for last in to_tokens(lambda t: kT[:, j, P * t:P * (t + 1)] if t < TT else kT[:, j, SEQ + PAST:NKEY],
                                      CH * j, kv_ev):
                    last.then_inc(kv_tr, 1)
            for j in range(NKV):
                n = N_KV + NKV + j
                pe.wait_ge(ev_act, n - 1)
                gemm(n, n % 2, xa)
                pe.wait_ge(ev_act, n + 1)
                pe.wait_ge(kv_ev, CH * (NKV + j))
                for last in to_tokens(lambda t: st[:, 0, P * t:P * t + rows(t)], CH * (NKV + j), kv_ev):
                    last.then_inc(kv_tr, 1)
            pe.wait_ge(kv_ev, CH * 2 * NKV)
            with pe.Fori(0, H // 2) as i:
                for j in range(2):
                    pe.wait_ge(ev_act, 2 * i + (N_Q + j - 1))
                    gemm(2 * i + (N_Q + j), (N_Q + j) % 2, xa)
                    head_means(2 * i + (NKV + j))

            pe.wait_ge(ev_act, N_GLU)
            pe.wait_ge(ki_ok, 1)
            pe.wait_ge(qk_rt, CH * (NKV + H))
            for i, (t, c, w, h) in enumerate(SCORES):
                wait(pe, sc_relu, i - 1)
                half = IDIM * (h % 2)
                nc.tensor.matmul(aux[0:rows(t), i % 2, 0:w], qiT[half:half + IDIM, h // 2, P * t:P * t + rows(t)],
                                 kiT[half:half + IDIM, kcol(t) + c:kcol(t) + c + w], start=True, stop=True).then_inc(sc_mm, 1)
            pe.wait_ge(sc_relu, NSC)
            pe.wait_ge(hist_ld, 16)
            for k in range(KT):
                last = nc.tensor.transpose(aux[:, 0, 32 * k:32 * k + HIST], st[0:HIST, 2, P * k:P * (k + 1)],
                                           ident[0:HIST, 0:HIST])
            last.then_inc(hist_tr, 1)
            gemm_pairs(N_GLU, 2 * KT, xa, ev_act, N_GLU)
            pe.wait_ge(hist_ok, 1)
            with pe.Fori(0, (N_VG - N_GATE) // 2) as i:
                for j in range(2):
                    pe.wait_ge(ev_act, 2 * i + (N_GATE + j - 1))
                    gemm(2 * i + (N_GATE + j), (N_GATE + j) % 2, xa)
                    modulate(i, j)

            def layer_norm_sums(src, nth):
                for k in range(KT):
                    for c in range(CH):
                        nc.tensor.matmul(acc[:, 0, c, 0:CW], mean_d[:, :], src[:, k, CW * c:CW * (c + 1)],
                                         start=(k == 0), stop=(k == KT - 1))
                    pe.wait_ge(ln_sq, KT * nth + k + 1)
                    for c in range(CH):
                        last = nc.tensor.matmul(acc[:, 1, c, 0:CW], mean_d[:, :], st[:, k % 2, CW * c:CW * (c + 1)],
                                                start=(k == 0), stop=(k == KT - 1))
                    last.then_inc(ln_mm, 1)

            pe.wait_ge(conv_ok, KT)
            pe.wait_ge(ev_act, N_VG)
            pe.wait_ge(mod_ok, 4)
            for m in range(4):
                if m >= 2:
                    pe.wait_ge(tail_ev, m - 1)
                for k in range(4):
                    last = nc.tensor.transpose(aux[0:HIST, m % 2, P * k:P * (k + 1)], ctail[:, 4 * (m % 2) + k, m // 2, :],
                                               ident[:, :])
                last.then_inc(tail_tr, 1)
            layer_norm_sums(apad, 0)
            pe.wait_ge(ln_ok, 1)
            gemm_pairs(N_VG, KT, xa, ev_act, N_VG)
            pe.wait_ge(ev_act, N_PC)
            pe.wait_ge(v_add, 2 * KT + 2)
            for m in range(2):
                for c in range(CH):
                    last = nc.tensor.matmul(acc[:, m, c, 0:CW], mean_d[:, :], st[:, 4 * m, CW * c:CW * (c + 1)],
                                            start=True, stop=True)
            last.then_inc(ln_mm, 1)
            pe.wait_ge(ln_ok, 2)
            pe.wait_ge(tail_ev, 4)
            pe.wait_ge(bs_ld, 16)
            pe.wait_ge(ws_ok, 1)

            def transposed(i, j, m):
                if m == 0:
                    pe.wait_ge(vg_ok, 2 * i + (j + 1))
                    wait(pe, vg_ev, 6 * i + 3 * j)
                if m == 2:
                    pe.wait_ge(vg_ev, 6 * i + (3 * j + 1))
                for q, t in enumerate((range(0, 4), range(4, 8), (TT,))[m]):
                    last = nc.tensor.transpose(aux[:, m % 2, P * q:P * (q + 1)], vgc[:, j % 2, P * t:P * (t + 1)], ident[:, :])
                last.then_inc(vg_tr, 1)

            def mix_pair(i, last_pair=False):
                for j in range(2):
                    more = not (last_pair and j)
                    if more:
                        transposed(i, j + 1, 0)
                        transposed(i, j + 1, 1)
                    g = bass.ds(2 * i + j, 1)
                    pe.wait_ge(vg_ev, 6 * i + (3 * j + 3))
                    wait(pe, mix_ev, 6 * i + 3 * (j - 1))
                    for m, tiles in enumerate((range(0, 4), range(4, 8), (TT,))):
                        for q, t in enumerate(tiles):
                            r = rows(t)
                            out = acc[:, j, m, P * q:P * q + r]
                            nc.tensor.matmul(out, vgt[:, j, P * t:P * (t + 1)], wmT[:, g, 0:r], start=True, stop=False)
                            last = nc.tensor.matmul(out, ones_row[:, :], bs_row[:, g, 0:r], start=False, stop=True)
                        last.then_inc(mix_mm, 1)
                        if more and m == 0:
                            transposed(i, j + 1, 2)

            for m in range(3):
                transposed(0, 0, m)
            mix_pair(0)
            with pe.Fori(1, KT // 2 - 1) as i:
                mix_pair(i)
            mix_pair(KT // 2 - 1, last_pair=True)

            pe.wait_ge(ev_act, N_PC)
            pe.wait_ge(mix_ev, CH * KT)

            def logits(a, h):
                t, n = ATT[a]
                r, w, i = rows(t), WIDTH[t], G * a + h
                if i % H == 0:
                    pe.wait_ge(q_ld[t % 2], 16 * (t // 2 + 1))
                wait(pe, lg_ev, i - 1)
                for c in range(0, w, 512):
                    last = nc.tensor.matmul(acc[0:r, h % 2, c // 512, 0:min(512, w - c)], (qt, qt2)[t % 2][:, i % H, 0:r],
                                            kT[:, n, kcol(t) + c:kcol(t) + min(c + 512, w)], start=True, stop=True)
                last.then_inc(lg_mm, 1)

            def transposes(a, b):
                t, _ = ATT[a]
                col, _, kr = key_tiles(t)[b]
                r, i = rows(t), FIRST[a] + b
                wait(pe, (pt_eva, pt_evd)[i % 2], i // 2)
                for h in range(G):
                    if b == 0:
                        pe.wait_ge(pr_ok, G * a + h + 1)
                    last = nc.tensor.transpose(aux[0:kr, i % 2, r * h:r * (h + 1)], probs(a, h)[:, col:col + kr],
                                               ident[0:r, 0:r])
                last.then_inc(pt_tr, 1)

            def values(a, b):
                t, n = ATT[a]
                kts = key_tiles(t)
                _, kt, kr = kts[b]
                r, i = rows(t), FIRST[a] + b
                pe.wait_ge((pt_eva, pt_evd)[i % 2], i // 2 + 1)
                if b == 0:
                    wait(pe, o_lo, a - 1)
                nc.tensor.matmul(acc[:, n, 2, 0:G * r], vtok[0:kr, kt, DH * n:DH * (n + 1)],
                                 st[0:kr, 4, 512 * (i % 2):512 * (i % 2) + G * r],
                                 start=(b == 0), stop=(b == len(kts) - 1)).then_inc(pv_mm, 1)

            for nxt, h, a, blocks in attention_steps():
                if nxt is not None:
                    logits(nxt, h)
                for b in blocks:
                    transposes(a, b)
                    if b:
                        values(a, b - 1)
                if a >= 0 and h == G - 1:
                    values(a, FIRST[a + 1] - FIRST[a] - 1)

            pe.wait_ge(o_lo, len(ATT))
            pe.wait_ge(xa_ok, 2)
            gemm_pairs(N_PC, KT, xa, ev_dve, 0)
            gemm_pairs(N_PB, KT, xb, ev_dve, KT, br_lo, 0)
            gemm_pairs(N_PA, KT, xa, ev_dve, 2 * KT, br_lo, KT)
            gemm_pairs(N_WO, KT, xb, ev_dve, 3 * KT, m_lo, 0)
            pe.wait_ge(sq_add, KT + 1)
            for c in range(CH):
                last = nc.tensor.matmul(acc[:, 1, c, 0:CW], mean_d[:, :], st[:, 2, CW * c:CW * (c + 1)],
                                        start=True, stop=True)
            last.then_inc(sq_mm, 1)
            pe.wait_ge(rt_ok, 2)
            gemm_as_ready(N_MLP, N_MLP % 2, xb, h_lo, KT)

            def hidden_group(g, first, last):
                n = N_GRP
                for j in range(1, FG + 1 - last):
                    if j <= 2 and not (first and j == 2):
                        if not first:
                            pe.wait_ge(ev_dve, KT * g + (4 * KT + j - 2))
                    else:
                        pe.wait_ge(ev_act, FG * g + (N_PC + j - 1))
                    gemm(GT * g + n, n % 2, xb)
                    n += 1
                for j in range(KT):
                    if j < 2:
                        pe.wait_ge(ev_act, FG * g + (N_PC + FG - last + j))
                    else:
                        pe.wait_ge(ev_dve, KT * g + (4 * KT + j - 1))
                    if j == 0:
                        pe.wait_ge(f_lo, FG * g + FG)
                    gemm(GT * g + n, n % 2, xf, nk=FG)
                    n += 1

            hidden_group(0, True, 0)
            with pe.Fori(1, NG - 1) as g:
                hidden_group(g, False, 0)
            hidden_group(NG - 1, False, 1)
            pe.wait_ge(ev_dve, (4 + NG) * KT)
            for t in range(TT + 1):
                r = rows(t)
                for half, done in ((0, y_eva), (1, y_evd)):
                    wait(pe, done, t)
                    for k in range(4):
                        last = nc.tensor.transpose(aux[0:r, half, P * k:P * (k + 1)], x1T[:, 4 * half + k, P * t:P * t + r],
                                                   ident[:, :])
                    last.then_inc(y_tr, 1)


_INS = ['x_prompt', 'x_sample', 'c_prompt', 'c_sample', 'cache_k', 'cache_v', 'cache_kidx', 'cache_conv',
        'w_ada', 'b_ada', 'g_norm1', 'w_in', 'w_dw', 'b_dw', 'ln_c_g', 'ln_c_b', 'w_pa', 'ln_v_g', 'ln_v_b',
        'w_s', 'b_s', 'w_pb', 'g_q', 'g_k', 'w_pc', 'w_o', 'g_norm2', 'w_1', 'b_1', 'w_2', 'b_2']
_OUTS = [(1, SEQ, D), (1, DEC, D),
         (1, 1, SEQ, NKV, DH), (1, 1, SEQ, NKV, DH), (1, 1, SEQ, IDIM), (1, 1, HIST, D),
         (1, 1, DEC, NKV, DH), (1, 1, DEC, NKV, DH), (1, 1, DEC, IDIM), (1, 1, HIST, D), (1, 1, DEC, D)]


def kernel(**inputs):
    import numpy as _np
    import concourse.bacc as _bacc
    from concourse import mybir as _mybir
    from concourse.bass_utils import run_bass_kernel_spmd as _run

    nc = _bacc.Bacc("TRN2", target_bir_lowering=False, num_devices=1)
    arrays, args = {}, []
    for name in _INS:
        a = _np.ascontiguousarray(inputs[name])
        arrays[f"in_{name}_dram"] = a
        args.append(nc.dram_tensor(f"in_{name}_dram", a.shape, _mybir.dt.from_np(a.dtype), kind="ExternalInput").ap())
    for i, shape in enumerate(_OUTS):
        args.append(nc.dram_tensor(f"out_{i}_dram", shape, _mybir.dt.float32, kind="ExternalOutput").ap())
    hybrid_stream_step(nc, *args)
    r = _run(nc, [arrays], core_ids=[0])
    return tuple(r.results[0][f"out_{i}_dram"] for i in range(len(_OUTS)))
```
